# Optimizing a Trainium2 kernel written in Bass

```python
import math
import jax, jax.numpy as jnp
from jax import lax
import numpy as np

D_MODEL = 1024
BATCH = 1
SEQ = 1024
DEPTH = 2
DEC_BATCH = 8
DEC_SEQ = 1
PAST_LEN = 4096
PAGE_SIZE = 128

HEAD_DIM = 64
ROT_DIM = HEAD_DIM // 4
ROPE_THETA = 500000.0
DILATED_GROUPS = ((128, 1), (512, 4), (2048, 16))
N_GROUPS_A = len(DILATED_GROUPS)
N_HEADS_A = D_MODEL // HEAD_DIM
N_HEADS_B = D_MODEL // HEAD_DIM
N_KV_HEADS_B = 2
GQA_B = N_HEADS_B // N_KV_HEADS_B
WINDOW_B = 128
BLOCK_B = 128
D_FF = 2816
CONV_W = 3
N_MIXERS = 2
N_LAYERS_A = (DEPTH + 1) // 2
N_LAYERS_B = DEPTH // 2
ALPHA = (2.0 * DEPTH) ** 0.25
BETA = (8.0 * DEPTH) ** -0.25
LN_EPS = 1e-5
NEG_INF = -1e30
SCALE = 1.0 / math.sqrt(HEAD_DIM)

kernel_name = "hybrid_dilated_swa_sink_convffn_step"

def rope(x, pos):
    half = ROT_DIM // 2
    inv_freq = ROPE_THETA ** (-jnp.arange(half, dtype=jnp.float32) * 2.0 / ROT_DIM)
    ang = pos.astype(jnp.float32)[:, None] * inv_freq[None, :]
    ang = ang.reshape((ang.shape[0],) + (1,) * (x.ndim - 3) + (half,))
    cos, sin = jnp.cos(ang), jnp.sin(ang)
    x1, x2, rest = x[..., :half], x[..., half:ROT_DIM], x[..., ROT_DIM:]
    return jnp.concatenate([(x1 * cos - x2 * sin).astype(x.dtype),
                            (x2 * cos + x1 * sin).astype(x.dtype), rest], axis=-1)

def layer_norm(x, g, b):
    xf = x.astype(jnp.float32)
    mu = xf.mean(-1, keepdims=True)
    var = jnp.square(xf - mu).mean(-1, keepdims=True)
    return ((xf - mu) * lax.rsqrt(var + LN_EPS) * g + b).astype(x.dtype)

def band_pair(xb):
    prev = jnp.concatenate([jnp.zeros_like(xb[:, :1]), xb[:, :-1]], axis=1)
    return jnp.concatenate([prev, xb], axis=2)

def masked_softmax_lse(s, mask):
    s = jnp.where(mask, s, NEG_INF)
    m = s.max(axis=-1, keepdims=True)
    e = jnp.exp(s - m)
    den = e.sum(axis=-1, keepdims=True)
    return e / den, (m + jnp.log(den))[..., 0]

def sink_softmax(s, mask, sinks):
    sink = sinks.astype(jnp.float32).reshape((1, N_KV_HEADS_B, GQA_B) + (1,) * (s.ndim - 3))
    s = jnp.where(mask, s, NEG_INF)
    m = jnp.maximum(s.max(axis=-1, keepdims=True), sink)
    e = jnp.exp(s - m)
    return e / (e.sum(axis=-1, keepdims=True) + jnp.exp(sink - m))

def merge_by_denominator(outs, lses):
    o = jnp.stack(outs)
    w = jax.nn.softmax(jnp.stack(lses), axis=0)
    return jnp.sum(w[..., None] * o, axis=0)

def a_project(x, pos, w_qkv):
    B, T, _ = x.shape
    qkv = (x @ w_qkv).reshape(B, T, N_GROUPS_A, 3, N_HEADS_A, HEAD_DIM)
    return rope(qkv[:, :, :, 0], pos), rope(qkv[:, :, :, 1], pos), qkv[:, :, :, 2]

def dilated_band_attention(q, k, v, win, dil):
    B, S, H, Dh = q.shape
    band = win // dil
    L = S // dil
    nb = -(-L // band)
    Lp = nb * band

    def to_classes(t):
        t = t.reshape(B, L, dil, H, Dh).transpose(0, 2, 1, 3, 4).reshape(B * dil, L, H, Dh)
        return jnp.pad(t, ((0, 0), (0, Lp - L), (0, 0), (0, 0))).reshape(B * dil, nb, band, H, Dh)

    qb = to_classes(q)
    kk = band_pair(to_classes(k))
    vv = band_pair(to_classes(v))
    s = jnp.einsum('nbqhd,nbphd->nhbqp', qb, kk).astype(jnp.float32) * SCALE
    i = jnp.arange(band)[:, None]
    p = jnp.arange(2 * band)[None, :]
    dist = band + i - p
    blk = jnp.arange(nb)[:, None, None]
    mask = (dist >= 0) & (dist <= band) & ((blk > 0) | (p >= band))
    probs, lse = masked_softmax_lse(s, mask)
    o = jnp.einsum('nhbqp,nbphd->nbqhd', probs, vv)
    o = o.reshape(B, dil, Lp, H, Dh)[:, :, :L].transpose(0, 2, 1, 3, 4).reshape(B, S, H, Dh)
    lse = lse.transpose(0, 2, 3, 1).reshape(B, dil, Lp, H)[:, :, :L].transpose(0, 2, 1, 3).reshape(B, S, H)
    return o, lse

def mixer_a_prompt(x, pos, w_qkv, w_o):
    B, S, _ = x.shape
    q, k, v = a_project(x, pos, w_qkv)
    outs, lses, states = [], [], []
    for g, (win, dil) in enumerate(DILATED_GROUPS):
        o, lse = dilated_band_attention(q[:, :, g], k[:, :, g], v[:, :, g], win, dil)
        outs.append(o)
        lses.append(lse)
        keep = min(win, S)
        states.append(jnp.stack([k[:, S - keep:, g], v[:, S - keep:, g]], axis=1))
    y = merge_by_denominator(outs, lses).astype(x.dtype).reshape(B, S, N_HEADS_A * HEAD_DIM) @ w_o
    return y, states

def mixer_a_sample(x, pos, bufs, w_qkv, w_o):
    B, T, _ = x.shape
    q, k, v = a_project(x, pos, w_qkv)
    outs, lses, states = [], [], []
    for g, (win, dil) in enumerate(DILATED_GROUPS):
        buf = bufs[g]
        L = buf.shape[2]
        new_st = jnp.concatenate([buf[:, :, T:], jnp.stack([k[:, :, g], v[:, :, g]], axis=1)], axis=2)
        idx = L + jnp.arange(T)[:, None] - dil * jnp.arange(win // dil + 1)[None, :]
        valid = idx >= 0
        in_head = (idx < T)[None, None, :, :, None, None]
        g_head = buf[:, :, jnp.clip(idx, 0, T - 1)]
        g_tail = new_st[:, :, jnp.clip(idx - T, 0, L - 1)]
        kvg = jnp.where(in_head, g_head, g_tail)
        s = jnp.einsum('bthd,btkhd->bhtk', q[:, :, g], kvg[:, 0]).astype(jnp.float32) * SCALE
        probs, lse = masked_softmax_lse(s, valid[None, None])
        outs.append(jnp.einsum('bhtk,btkhd->bthd', probs, kvg[:, 1]))
        lses.append(lse.transpose(0, 2, 1))
        states.append(new_st)
    y = merge_by_denominator(outs, lses).astype(x.dtype).reshape(B, T, N_HEADS_A * HEAD_DIM) @ w_o
    return y, states

def b_project(x, pos, w_qkv, b_qkv):
    B, T, _ = x.shape
    qkv = x @ w_qkv + b_qkv
    nq = N_HEADS_B * HEAD_DIM
    nkv = N_KV_HEADS_B * HEAD_DIM
    q = rope(qkv[..., :nq].reshape(B, T, N_KV_HEADS_B, GQA_B, HEAD_DIM), pos)
    k = rope(qkv[..., nq:nq + nkv].reshape(B, T, N_KV_HEADS_B, HEAD_DIM), pos)
    v = qkv[..., nq + nkv:].reshape(B, T, N_KV_HEADS_B, HEAD_DIM)
    return q, k, v

def mixer_b_prompt(x, pos, w_qkv, b_qkv, sinks, w_o, b_o):
    B, S, _ = x.shape
    q, k, v = b_project(x, pos, w_qkv, b_qkv)
    nb = S // BLOCK_B
    qb = q.reshape(B, nb, BLOCK_B, N_KV_HEADS_B, GQA_B, HEAD_DIM)
    kk = band_pair(k.reshape(B, nb, BLOCK_B, N_KV_HEADS_B, HEAD_DIM))
    vv = band_pair(v.reshape(B, nb, BLOCK_B, N_KV_HEADS_B, HEAD_DIM))
    s = jnp.einsum('bnqhgd,bnphd->bhgnqp', qb, kk).astype(jnp.float32) * SCALE
    i = jnp.arange(BLOCK_B)[:, None]
    p = jnp.arange(2 * BLOCK_B)[None, :]
    dist = BLOCK_B + i - p
    blk = jnp.arange(nb)[:, None, None]
    mask = (dist >= 0) & (dist < WINDOW_B) & ((blk > 0) | (p >= BLOCK_B))
    probs = sink_softmax(s, mask, sinks)
    o = jnp.einsum('bhgnqp,bnphd->bnqhgd', probs, vv).astype(x.dtype).reshape(B, S, N_HEADS_B * HEAD_DIM)
    keep = min(WINDOW_B, S)
    return o @ w_o + b_o, jnp.stack([k[:, S - keep:], v[:, S - keep:]], axis=1)

def mixer_b_sample(x, pos, buf, w_qkv, b_qkv, sinks, w_o, b_o):
    B, T, _ = x.shape
    q, k, v = b_project(x, pos, w_qkv, b_qkv)
    L = buf.shape[2]
    kf = jnp.concatenate([buf[:, 0], k], axis=1)
    vf = jnp.concatenate([buf[:, 1], v], axis=1)
    s = jnp.einsum('bthgd,brhd->bhgtr', q, kf).astype(jnp.float32) * SCALE
    dist = L + jnp.arange(T)[:, None] - jnp.arange(L + T)[None, :]
    mask = (dist >= 0) & (dist < WINDOW_B)
    probs = sink_softmax(s, mask, sinks)
    o = jnp.einsum('bhgtr,brhd->bthgd', probs, vf).astype(x.dtype).reshape(B, T, N_HEADS_B * HEAD_DIM)
    return o @ w_o + b_o, jnp.stack([kf[:, T:], vf[:, T:]], axis=1)

def conv_ffn(x, prev, w_up, conv_w, conv_b, w_down):
    T = x.shape[1]
    gu = x @ w_up
    g, u = gu[..., :D_FF], gu[..., D_FF:]
    gfull = jnp.concatenate([prev.astype(g.dtype), g], axis=1)
    gc = conv_b + sum(conv_w[j] * gfull[:, j:j + T] for j in range(CONV_W))
    return (jax.nn.silu(gc) * u) @ w_down, gfull[:, T:]

def setup_inputs(seed: int = 0) -> dict:
    key = jax.random.key(seed)
    ks = jax.random.split(key, 24)
    f32 = jnp.float32

    def nrm(k, shape, scale):
        return jax.random.normal(k, shape, f32) * scale

    x_prompt = nrm(ks[0], (BATCH, SEQ, D_MODEL), 1.0)
    x_sample = nrm(ks[1], (DEC_BATCH, DEC_SEQ, D_MODEL), 1.0)
    cache_a1 = nrm(ks[2], (N_LAYERS_A, DEC_BATCH, 2, min(DILATED_GROUPS[0][0], PAST_LEN), N_HEADS_A, HEAD_DIM), 1.0)
    cache_a2 = nrm(ks[3], (N_LAYERS_A, DEC_BATCH, 2, min(DILATED_GROUPS[1][0], PAST_LEN), N_HEADS_A, HEAD_DIM), 1.0)
    cache_a3 = nrm(ks[4], (N_LAYERS_A, DEC_BATCH, 2, min(DILATED_GROUPS[2][0], PAST_LEN), N_HEADS_A, HEAD_DIM), 1.0)
    cache_b = nrm(ks[5], (N_LAYERS_B, DEC_BATCH, 2, min(WINDOW_B, PAST_LEN), N_KV_HEADS_B, HEAD_DIM), 1.0)
    state_ffn = nrm(ks[6], (DEPTH, DEC_BATCH, CONV_W - 1, D_FF), 1.0)
    wa = nrm(ks[7], (N_LAYERS_A, D_MODEL, N_GROUPS_A, 3, N_HEADS_A * HEAD_DIM), D_MODEL ** -0.5)
    w_qkv_a = (wa * jnp.array([1.0, 1.0, BETA], f32)[:, None]).reshape(N_LAYERS_A, D_MODEL, -1)
    w_o_a = nrm(ks[8], (N_LAYERS_A, N_HEADS_A * HEAD_DIM, D_MODEL), (N_HEADS_A * HEAD_DIM) ** -0.5 * BETA)
    col_scale_b = jnp.concatenate([jnp.ones(((N_HEADS_B + N_KV_HEADS_B) * HEAD_DIM,), f32),
                                   jnp.full((N_KV_HEADS_B * HEAD_DIM,), BETA, f32)])
    w_qkv_b = nrm(ks[9], (N_LAYERS_B, D_MODEL, (N_HEADS_B + 2 * N_KV_HEADS_B) * HEAD_DIM), D_MODEL ** -0.5) * col_scale_b
    b_qkv_b = nrm(ks[10], (N_LAYERS_B, (N_HEADS_B + 2 * N_KV_HEADS_B) * HEAD_DIM), 0.02)
    sinks_b = nrm(ks[11], (N_LAYERS_B, N_HEADS_B), 0.5)
    w_o_b = nrm(ks[12], (N_LAYERS_B, N_HEADS_B * HEAD_DIM, D_MODEL), (N_HEADS_B * HEAD_DIM) ** -0.5 * BETA)
    b_o_b = nrm(ks[13], (N_LAYERS_B, D_MODEL), 0.02)
    w_up = nrm(ks[14], (DEPTH, D_MODEL, 2 * D_FF), D_MODEL ** -0.5)
    conv_w = nrm(ks[15], (DEPTH, CONV_W, D_FF), 0.5)
    conv_b = nrm(ks[16], (DEPTH, D_FF), 0.02)
    w_down = nrm(ks[17], (DEPTH, D_FF, D_MODEL), D_FF ** -0.5 * BETA)
    ln_g = 1.0 + nrm(ks[18], (DEPTH, 2, D_MODEL), 0.02)
    ln_b = nrm(ks[19], (DEPTH, 2, D_MODEL), 0.02)
    return {"x_prompt": x_prompt, "x_sample": x_sample,
            "cache_a1": cache_a1, "cache_a2": cache_a2, "cache_a3": cache_a3,
            "cache_b": cache_b, "state_ffn": state_ffn,
            "w_qkv_a": w_qkv_a, "w_o_a": w_o_a,
            "w_qkv_b": w_qkv_b, "b_qkv_b": b_qkv_b, "sinks_b": sinks_b, "w_o_b": w_o_b, "b_o_b": b_o_b,
            "w_up": w_up, "conv_w": conv_w, "conv_b": conv_b, "w_down": w_down,
            "ln_g": ln_g, "ln_b": ln_b}

def reference(x_prompt, x_sample, cache_a1, cache_a2, cache_a3, cache_b, state_ffn,
              w_qkv_a, w_o_a, w_qkv_b, b_qkv_b, sinks_b, w_o_b, b_o_b,
              w_up, conv_w, conv_b, w_down, ln_g, ln_b):
    caches_a = (cache_a1, cache_a2, cache_a3)
    pos_p = jnp.arange(x_prompt.shape[1], dtype=jnp.int32)
    pos_s = PAST_LEN + jnp.arange(x_sample.shape[1], dtype=jnp.int32)
    xp, xs = x_prompt, x_sample
    new_a_p = [[] for _ in range(N_GROUPS_A)]
    new_a_s = [[] for _ in range(N_GROUPS_A)]
    new_b_p, new_b_s, new_f_p, new_f_s = [], [], [], []
    for i in range(DEPTH):
        j = i // N_MIXERS
        if i % N_MIXERS == 0:
            hp, st_p = mixer_a_prompt(xp, pos_p, w_qkv_a[j], w_o_a[j])
            hs, st_s = mixer_a_sample(xs, pos_s, [c[j] for c in caches_a], w_qkv_a[j], w_o_a[j])
            for g in range(N_GROUPS_A):
                new_a_p[g].append(st_p[g])
                new_a_s[g].append(st_s[g])
        else:
            hp, st_p = mixer_b_prompt(xp, pos_p, w_qkv_b[j], b_qkv_b[j], sinks_b[j], w_o_b[j], b_o_b[j])
            hs, st_s = mixer_b_sample(xs, pos_s, cache_b[j], w_qkv_b[j], b_qkv_b[j], sinks_b[j], w_o_b[j], b_o_b[j])
            new_b_p.append(st_p)
            new_b_s.append(st_s)
        xp = layer_norm(ALPHA * xp + hp, ln_g[i, 0], ln_b[i, 0])
        xs = layer_norm(ALPHA * xs + hs, ln_g[i, 0], ln_b[i, 0])
        zeros_prev = jnp.zeros((xp.shape[0], CONV_W - 1, D_FF), xp.dtype)
        fp, sp = conv_ffn(xp, zeros_prev, w_up[i], conv_w[i], conv_b[i], w_down[i])
        fs, ss = conv_ffn(xs, state_ffn[i], w_up[i], conv_w[i], conv_b[i], w_down[i])
        new_f_p.append(sp)
        new_f_s.append(ss)
        xp = layer_norm(ALPHA * xp + fp, ln_g[i, 1], ln_b[i, 1])
        xs = layer_norm(ALPHA * xs + fs, ln_g[i, 1], ln_b[i, 1])
    return (xp, xs,
            jnp.stack(new_a_p[0]), jnp.stack(new_a_s[0]),
            jnp.stack(new_a_p[1]), jnp.stack(new_a_s[1]),
            jnp.stack(new_a_p[2]), jnp.stack(new_a_s[2]),
            jnp.stack(new_b_p), jnp.stack(new_b_s),
            jnp.stack(new_f_p), jnp.stack(new_f_s))


_drawn_inputs = setup_inputs


def setup_inputs(seed=0):
    import zlib

    import numpy as np

    out = dict(_drawn_inputs(seed))
    spreads = {}
    factors = {'sinks_b': 25.268, 'b_o_b': 3.823, 'conv_b': 8.0}
    for name, (base, spread) in spreads.items():
        noise = np.random.default_rng([zlib.crc32(name.encode()), seed]).standard_normal(out[name].shape)
        drawn = base * np.exp(spread * noise) if base else spread * noise
        out[name] = __import__('jax').numpy.asarray(drawn.astype(out[name].dtype))
    for name, factor in factors.items():
        out[name] = (out[name] * factor).astype(out[name].dtype)
    return out
```

```python
import math
from contextlib import ExitStack

import numpy as np

import concourse.bass as bass
from concourse import mybir

F32 = mybir.dt.float32
F32R = mybir.dt.float32r
ALU = mybir.AluOpType
ACT = mybir.ActivationFunctionType
AX_X = mybir.AxisListType.X

P = 128
D = 1024
SEQ = 1024
NS = 8
T = SEQ + NS
PAST = 4096
HD = 64
NH = D // HD
ROT = HD // 4
THETA = 500000.0
GROUPS = ((128, 1), (512, 4), (2048, 16))
NG = len(GROUPS)
DIL = [d for _, d in GROUPS]
NKV_B = 2
GQA_B = NH // NKV_B
DFF = 2816
ALPHA = (2.0 * 2) ** 0.25
LN_EPS = 1e-5
SCALE = 1.0 / math.sqrt(HD)
BIG = 1e30

KT = D // P
PAIRS = NH // 2
QT = SEQ // P
FT = DFF // P
CHUNKS = ((0, 352), (352, 352), (704, T - 704))
NCH = len(CHUNKS)
CW = 352
KEYS = 128


def f32(ap):
    return ap.bitcast(F32)


def need(eng, sem, count):
    if isinstance(count, int) and count <= 0:
        return
    eng.wait_ge(sem, count)


def need_apart(eng, sem, count, steps):
    need(eng, sem, count)
    if not isinstance(count, int):
        eng.sem_inc(steps)


def semaphore(nc, name, sems):
    sems.append(nc.alloc_semaphore(name))
    return sems[-1]


def clear(nc, sems):
    nc.clear_and_free_semaphores(sems)
    nc.all_engine_barrier()


def take(ap, i):
    if isinstance(i, int):
        return ap[i]
    flat = ap[bass.ds(i, 1)]
    return flat.rearrange("o a b -> (o a) b") if len(ap.shape) == 3 else flat.rearrange("o a b c -> (o a) b c")


def span(i, n):
    return slice(i, i + n) if isinstance(i, int) else bass.ds(i, n)


def product(pe, out, w_hi, w_lo, x_hi, x_lo, first, last):
    pe.matmul(out, w_hi, x_hi, start=first, stop=False)
    pe.matmul(out, w_hi, x_lo, start=False, stop=False)
    return pe.matmul(out, w_lo, x_hi, start=False, stop=last)


def blocks_before(g, t):
    if g == 0:
        return 1 if t > 0 else 0
    if g == 1:
        return t % 2
    return 0


def class_major(ap, g):
    return ap.rearrange("p (i c) -> p c i", c=DIL[g])


def class_tiles(ap, g):
    return ap.rearrange("p (c i) -> p c i", c=DIL[g])


def tile_tokens(ap, g, t):
    if g == 0:
        return ap[:, t * P:(t + 1) * P]
    if g == 1:
        return class_major(ap, g)[:, t // 2, (t % 2) * P:(t % 2 + 1) * P]
    return class_major(ap, g)[:, 2 * t:2 * t + 2, :]


def tile_shape(ap, g):
    return ap.rearrange("p (c i) -> p c i", c=2) if g == 2 else ap


def mixer_a(nc, x_hi, x_lo, dram):
    ctx = ExitStack()
    sems = []
    with ctx:
        def sb(name, shape, dt=F32):
            return ctx.enter_context(nc.sbuf_tensor("a_" + name, shape, dt))

        def ps(name):
            return ctx.enter_context(nc.psum_tensor("a_" + name, [P, 512], F32))

        def sem(name):
            return semaphore(nc, "a_" + name, sems)

        raw = sb("raw", [P, 2, KT, P])
        w_hi = sb("w_hi", [P, 2, KT, P], F32R)
        w_lo = sb("w_lo", [P, 2, KT, P], F32R)
        kq_hi = sb("kq_hi", [P, 2, 2, SEQ], F32R)
        kq_lo = sb("kq_lo", [P, 2, 2, SEQ], F32R)
        v_hi = sb("v_hi", [P, QT, P], F32R)
        v_lo = sb("v_lo", [P, QT, P], F32R)
        vt = sb("vt", [P, T])
        vraw = sb("vraw", [P, 512])
        cos = sb("cos", [P, T])
        sin = sb("sin", [P, T])
        mask = sb("mask", [P, 2 * P])
        mask3 = sb("mask3", [P, P])
        ident = sb("ident", [P, P])
        ev = sb("ev", [P, 2, CW])
        rot = sb("rot", [P, CW])
        t2 = sb("t2", [P, CW])
        qp = sb("qp", [P, 2, CW])
        sp = sb("sp", [P, 2, 2 * P])
        pt_hi = sb("pt_hi", [P, 4 * P], F32R)
        pt_lo = sb("pt_lo", [P, 4 * P], F32R)
        o = sb("o", [P, 2, NG, T])
        fbm = sb("fbm", [P, NG, P])
        st = sb("st", [P, 96])
        stT = sb("stT", [96, P])
        sr = sb("sr", [16, 2, NG, P])
        mt = sb("mt", [16, P])
        dd = sb("dd", [16, NG, P])
        mw = sb("mw", [16, NG, P])
        fw = sb("fw", [16, NG, P])
        f_hi = sb("f_hi", [16, NG, P], F32R)
        f_lo = sb("f_lo", [16, NG, P], F32R)
        sel = sb("sel", [16, QT, P], F32R)

        gb = [ps(f"gemm{i}") for i in range(2)]
        s_bank = [ps(f"scores{i}") for i in range(2)]
        pt_bank = ps("probsT")
        pv_bank = ps("pv")
        fb_bank = ps("factors")
        v_bank = ps("vT")

        s_apart = sem("apart")
        s_const, s_xin, s_xhi, s_xlo, s_sel = (sem(x) for x in ("const", "xin", "xhi", "xlo", "selr"))
        w_in = [sem("w_in0"), sem("w_in1")]
        s_whi, s_wlo, s_gemm, s_evac = (sem(x) for x in ("whi", "wlo", "gemm", "evac"))
        s_shuf, s_t1, s_t2, s_qp, s_kqhi, s_kqlo = (sem(x) for x in ("shuf", "t1", "t2", "qp", "kqhi", "kqlo"))
        kq_out = [sem("kq_out0"), sem("kq_out1")]
        s_vout, s_vtr, s_vev, s_vhi, s_vlo = (sem(x) for x in ("vout", "vtr", "vev", "vhi", "vlo"))
        s_scores, s_masked, s_probs, s_ptr, s_pthi, s_ptlo, s_pv, s_oev = (
            sem(x) for x in ("scores", "masked", "probs", "ptr", "pthi", "ptlo", "pv", "oev"))
        s_sttr, s_stcp, s_stout, s_srin, s_dve, s_dd, s_mw, s_f, s_fb, s_fbm, s_fbr, s_oout = (
            sem(x) for x in ("sttr", "stcp", "stout", "srin", "dve", "dd", "mw", "f", "fb", "fbm", "fbr", "oout"))

        NI = PAIRS * NG
        NB = NI * 3

        def items(eng, body):
            body(0, -1)
            for k in range(6):
                body(0, k)
            with eng.Fori(1, 3) as it:
                for k in range(6):
                    body(it, k)
            for k in range(6):
                body(3, k)

        class Item:
            def __init__(self, it, k):
                self.it, self.k = it, k
                self.attends = k >= 0
                self.projects = not (isinstance(it, int) and it == 3 and k == 5)
                self.g, self.set, self.buf = k % NG, k // NG, k % 2
                k1 = (k + 1) % 6
                self.g1, self.buf1 = k1 % NG, k1 % 2
                self.merges = k >= 3 or not (isinstance(it, int) and it == 0)

            def n(self, per=1, c=0):
                return self.it * (6 * per) + (self.k * per + c)

            def n1(self, per=1, c=0):
                return self.n(per, per + c)

            def p(self, per=1, c=0):
                return self.it * (2 * per) + (self.set * per + c)

            def p1(self, per=1, c=0):
                k1 = self.k + 1
                return self.it * (2 * per) + ((k1 // NG) * per + c)

            def parity(self, per, c):
                return ((self.k + 1) * per + c) % 2

        ctx.callback(clear, nc, sems)
        block = ctx.enter_context(nc.Block())

        @block.sync
        def _(sp_e):
            def load_block(b_expr, par):
                sp_e.dma_start(raw[:, par], take(dram["w_a"], b_expr).rearrange("p (k c) -> p k c", k=KT)
                               ).then_inc(w_in[par], 16)

            load_block(0, 0)
            for i in range(6):
                sp_e.dma_start(o[:, i // NG, i % NG, :], dram["xT"][i * P:(i + 1) * P, :]).then_inc(s_xin, 16)
                sp_e.wait_ge(s_xin, 16 * (i + 1)) if i == 5 else None
            load_block(1, 1)
            for dst, name in ((cos, "cos"), (sin, "sin"), (mask, "mask_a"), (mask3, "mask_c"), (ident, "ident")):
                sp_e.dma_start(dst[:, :], dram[name]).then_inc(s_const, 16)
            sp_e.dma_start(vt[0:16, 0:QT * P], dram["sel"]).then_inc(s_const, 16)
            sp_e.wait_ge(s_wlo, 1)
            load_block(2, 0)
            for i in range(6, KT):
                sp_e.wait_ge(s_xlo, i - 5)
                sp_e.dma_start(o[:, 0, i - 6, :], dram["xT"][i * P:(i + 1) * P, :]).then_inc(s_xin, 16)
                sp_e.wait_ge(s_xin, 16 * (i + 1))

            def send_stats(q):
                need_apart(sp_e, s_stcp, q, s_apart)
                need(sp_e, s_f, q - 1)
                sp_e.dma_start(dram["st_scr"], stT[:, :]).then_inc(s_stout, 16)
                need(sp_e, s_stout, q * 16)
                for w in range(2):
                    src = dram["st_scr"][w * 48:(w + 1) * 48, :].rearrange("(g h j) i -> g (h j i)", g=NG, h=2)
                    sp_e.dma_start(sr[:, w, 0, :], src[0].rearrange("(r i) -> r i", i=P)).then_inc(s_srin, 16)
                    for h in range(2):
                        row = src[1, h * SEQ:(h + 1) * SEQ].rearrange("(c b j i) -> b j c i", c=4, b=2, i=32)
                        for b in range(2):
                            sp_e.dma_start(
                                sr[8 * h + 4 * b:8 * h + 4 * b + 4, w, 1, :].rearrange("j (c i) -> j c i", c=4),
                                row[b]).then_inc(s_srin, 16)
                        row = src[2, h * SEQ:(h + 1) * SEQ].rearrange("(c j i) -> j c i", c=16, i=8)
                        sp_e.dma_start(sr[8 * h:8 * h + 8, w, 2, :].rearrange("j (c i) -> j c i", c=16),
                                       row).then_inc(s_srin, 16)

            def store_merged(q_rows, par, q):
                need(sp_e, s_fbr, q)
                sp_e.dma_start(dram["o_scr"][q_rows, 0:SEQ], o[:, par, 0, 0:SEQ]).then_inc(s_oout, 16)

            def body(it, k):
                m = Item(it, k)
                for t in range(9):
                    if m.attends and t == 0:
                        need(sp_e, s_evac, m.n(9, 9))
                        sp_e.dma_start(dram["vT"][m.g][span(m.p(P), P), :], vt[:, :]).then_inc(s_vout, 16)
                    if m.projects and t in (1, 4, 7):
                        c3 = t // 3 + 3
                        if not (isinstance(it, int) and m.n1(3, c3) >= NB):
                            need(sp_e, s_wlo, m.n1(3, c3 - 1))
                            load_block(m.n1(3, c3), m.parity(3, c3))
                    if m.projects and t - 1 in (0, 1, 2, 5):
                        s = t - 1
                        off, width = CHUNKS[s % 3]
                        need(sp_e, s_qp, m.n1(6, s + 1))
                        if s < 3:
                            sp_e.dma_start(dram["kT"][m.g1][span(m.p1(P), P), off:off + width],
                                           qp[:, s % 2, 0:width]).then_inc(kq_out[s % 2], 16)
                        else:
                            sp_e.dma_start(dram["q_s"][m.g1][span(m.p1(P), P), :],
                                           qp[:, s % 2, width - NS:width]).then_inc(kq_out[s % 2], 16)
                    if m.attends and m.merges and m.g == 0 and t == 2:
                        send_stats(m.p())
                    if m.attends and m.merges and m.g == 2 and t == 0:
                        store_merged(span(m.p(P, -P), P), 1 - m.set, m.p(8))
            items(sp_e, body)
            send_stats(PAIRS)
            store_merged(span((PAIRS - 1) * P, P), (PAIRS - 1) % 2, 8 * PAIRS)
            sp_e.wait_ge(s_oout, 16 * PAIRS)
            sp_e.wait_ge(s_vout, 16 * NI)
            sp_e.wait_ge(kq_out[0], 32 * NI)
            sp_e.wait_ge(kq_out[1], 32 * NI)

        @block.scalar
        def _(act):
            def split_w(par, count, chunks):
                act.wait_ge(w_in[par], count)
                need(act, s_gemm, chunks)
                act.copy(w_hi[:, par], raw[:, par]).then_inc(s_whi, 1)

            split_w(0, 16, 0)
            for i in range(KT):
                act.wait_ge(s_xin, 96 if i < 6 else 16 * (i + 1))
                act.copy(x_hi[:, i, :], o[:, (i % 6) // NG, i % NG, :]).then_inc(s_xhi, 1)

            def copy_stats(q):
                need(act, s_sttr, q)
                need(act, s_stout, q * 16 + (-16))
                act.copy(stT[:, :], fb_bank[0:96, 0:P]).then_inc(s_stcp, 1)

            def weigh(q):
                need(act, s_dd, q)
                act.activation(mw[:, :, :], dd[:, :, :], ACT.Exp).then_inc(s_mw, 1)

            def body(it, k):
                m = Item(it, k)
                for t in range(9):
                    if m.attends and t < 8:
                        if m.merges and m.g == 0 and t == 0:
                            copy_stats(m.p())
                        w0 = (1 - blocks_before(m.g, t)) * P
                        for h in range(2):
                            need(act, s_masked, m.n(16, 2 * t + h + 1))
                            c = m.g * 16 + h * 8 + t
                            act.activation(sp[:, h, w0:], sp[:, h, w0:], ACT.Exp, bias=st[:, c:c + 1], scale=-1.0,
                                           accum_out=st[:, 48 + c:49 + c]).then_inc(s_probs, 1)
                        if t < 2:
                            need(act, s_vtr, m.n(2, t + 1))
                            need(act, s_vlo, m.n(2, t))
                            act.copy(vraw[:, :], v_bank[:, :]).then_inc(s_vev, 1)
                        if m.merges and m.g == 0 and t == 5:
                            weigh(m.p())
                    if m.projects and 1 <= t <= 6:
                        s = t - 1
                        off, width = CHUNKS[s % 3]
                        n = min(width, SEQ - off)
                        need(act, s_qp, m.n1(6, s + 1))
                        dst = kq_hi[:, m.buf1, s // 3, :]
                        a, b = off // DIL[m.g1], (off + n) // DIL[m.g1]
                        act.copy(class_tiles(dst, m.g1)[:, :, a:b],
                                 class_major(qp[:, s % 2, 0:n], m.g1)).then_inc(s_kqhi, 1)
                    if m.projects and t in (1, 4, 7):
                        c1 = t // 3 + 1
                        if not (isinstance(it, int) and m.n1(3, c1) >= NB):
                            half = ((m.k + 1) * 3 + c1) // 2
                            split_w(m.parity(3, c1), it * (9 * 16) + 16 * (half + 1), m.n1(9, 3 * (c1 - 1)))
                    if m.projects:
                        off, width = CHUNKS[t % 3]
                        if t == 6:
                            need(act, s_vout, m.n1(16))
                            if k == -1:
                                act.wait_ge(s_sel, 1)
                        elif t < 6:
                            need(act, s_qp, m.n1(6, t - 1))
                        need(act, s_gemm, m.n1(9, t + 1))
                        bank = gb[m.parity(9, t)]
                        if t < 3:
                            act.copy(ev[:, t % 2, 0:width], bank[:, 0:width]).then_inc(s_evac, 1)
                        elif t < 6:
                            act.mul(ev[:, t % 2, 0:width], bank[:, 0:width], -SCALE).then_inc(s_evac, 1)
                        else:
                            n = min(width, SEQ - off)
                            if n < width:
                                act.copy(vt[:, SEQ:T], bank[:, n:width])
                            a, b = off // DIL[m.g1], (off + n) // DIL[m.g1]
                            act.copy(class_tiles(vt[:, 0:SEQ], m.g1)[:, :, a:b],
                                     class_major(bank[:, 0:n], m.g1)).then_inc(s_evac, 1)
                    if m.attends and t >= 1:
                        need(act, s_pv, m.n(8, t))
                        if m.g == 0 and t == 1:
                            need(act, s_oout, m.p(16, -16))
                        for h in range(2):
                            rows = slice(64 * h, 64 * h + 64)
                            last = act.copy(tile_tokens(o[rows, m.set, m.g, 0:SEQ], m.g, t - 1),
                                            tile_shape(pv_bank[rows, h * P:(h + 1) * P], m.g))
                        last.then_inc(s_oev, 1)
                    if m.attends and t < 8:
                        c0 = (1 - blocks_before(m.g, t)) * 2 * P
                        need(act, s_ptr, m.n(8, t + 1))
                        act.copy(pt_hi[:, c0:], pt_bank[:, c0:]).then_inc(s_pthi, 1)
            items(act, body)
            copy_stats(PAIRS)
            weigh(PAIRS)

        @block.gpsimd
        def _(pool):
            def body(it, k):
                m = Item(it, k)
                for t in range(9):
                    if m.attends and t < 2:
                        need_apart(pool, s_vev, m.n(2, t + 1), s_apart)
                        dst = slice(4 * t, 4 * t + 4)
                        pool.tensor_copy(v_hi[:, dst, :].rearrange("p a b -> p (a b)"), vraw[:, :]).then_inc(s_vhi, 1)
                        need(pool, s_vhi, m.n(2, t + 1))
                        pool.tensor_tensor(v_lo[:, dst, :].rearrange("p a b -> p (a b)"), vraw[:, :],
                                           f32(v_hi[:, dst, :].rearrange("p a b -> p (a b)")),
                                           ALU.subtract).then_inc(s_vlo, 1)
                    if m.projects and 1 <= t <= 6:
                        s = t - 1
                        off, width = CHUNKS[s % 3]
                        n = min(width, SEQ - off)
                        need(pool, s_evac, m.n1(9, s + 1))
                        if k == -1 and t == 1:
                            pool.wait_ge(s_const, 16 * 6)
                        pool.tensor_tensor(t2[:, 0:width], ev[:, s % 2, 0:width], cos[:, off:off + width],
                                           ALU.mult).then_inc(s_t2, 1)
                        need(pool, s_t1, m.n1(6, s + 1))
                        need(pool, s_t2, m.n1(6, s + 1))
                        need(pool, s_kqhi, m.n1(6, s - 1))
                        need(pool, kq_out[s % 2], m.n1(32, {0: 0, 1: 0, 2: 16, 3: 16, 4: 32, 5: 16}[s]))
                        pool.tensor_tensor(qp[:, s % 2, 0:width], rot[:, 0:width], t2[:, 0:width],
                                           ALU.add).then_inc(s_qp, 1)
                        need(pool, s_kqhi, m.n1(6, s + 1))
                        a, b = off // DIL[m.g1], (off + n) // DIL[m.g1]
                        hi = class_tiles(kq_hi[:, m.buf1, s // 3, :], m.g1)[:, :, a:b]
                        lo = class_tiles(kq_lo[:, m.buf1, s // 3, :], m.g1)[:, :, a:b]
                        need(pool, s_qp, m.n1(6, s + 1))
                        pool.tensor_tensor(lo, class_major(qp[:, s % 2, 0:n], m.g1), f32(hi),
                                           ALU.subtract).then_inc(s_kqlo, 1)
            items(pool, body)

        @block.vector
        def _(dve):
            swap = [i ^ (ROT // 2) if i < ROT else i for i in range(32)]

            def split_w(par, b1):
                need(dve, s_whi, b1)
                dve.tensor_tensor(w_lo[:, par], raw[:, par], f32(w_hi[:, par]), ALU.subtract).then_inc(s_wlo, 1)

            split_w(0, 1)
            for i in range(KT):
                dve.wait_ge(s_xhi, i + 1)
                dve.tensor_tensor(x_lo[:, i, :], o[:, (i % 6) // NG, i % NG, :], f32(x_hi[:, i, :]),
                                  ALU.subtract).then_inc(s_xlo, 1)
            dve.wait_ge(s_const, 16 * 6)
            dve.tensor_copy(sel[:, :, :].rearrange("r j f -> r (j f)"), vt[0:16, 0:QT * P]).then_inc(s_sel, 1)

            def natural(ap3, g):
                return ap3[:, g, :] if g == 0 else ap3[:, g, :].rearrange("r (c i) -> r i c", c=DIL[g])

            def plain(ap, g):
                return ap if g == 0 else ap.rearrange("r (i c) -> r i c", c=DIL[g])

            def step(q, idx, ins):
                ins.then_inc(s_dve, 1)
                need(dve, s_dve, q * 8 + (idx + 1 - 8))

            def differences(q):
                need(dve, s_srin, q * (16 * 14))
                nm, idx = sr[:, 0], 0
                step(q, 0, dve.tensor_tensor(plain(mt[:, :], 1), plain(nm[:, 0, :], 1), natural(nm, 1), ALU.min))
                step(q, 1, dve.tensor_tensor(plain(mt[:, :], 2), plain(mt[:, :], 2), natural(nm, 2), ALU.min))
                for g in range(NG):
                    last = dve.tensor_tensor(plain(dd[:, g, :], g), plain(mt[:, :], g), natural(nm, g), ALU.subtract)
                last.then_inc(s_dd, 1)

            def factors(q):
                need(dve, s_mw, q)
                den = sr[:, 1]
                for g in range(NG):
                    last = dve.tensor_tensor(plain(dd[:, g, :], g), plain(mw[:, g, :], g), natural(den, g), ALU.mult)
                step(q, 2, last)
                step(q, 3, dve.tensor_tensor(mt[:, :], dd[:, 0, :], dd[:, 1, :], ALU.add))
                step(q, 4, dve.tensor_tensor(mt[:, :], mt[:, :], dd[:, 2, :], ALU.add))
                step(q, 5, dve.reciprocal(mt[:, :], mt[:, :]))
                for g in range(NG):
                    last = dve.tensor_tensor(fw[:, g, :], mw[:, g, :], mt[:, :], ALU.mult)
                step(q, 6, last)
                need(dve, s_fb, q * 8 + (-8))
                step(q, 7, dve.tensor_copy(f_hi[:, :, :], fw[:, :, :]))
                dve.tensor_tensor(f_lo[:, :, :], fw[:, :, :], f32(f_hi[:, :, :]), ALU.subtract).then_inc(s_f, 1)

            def merge_tile(q, par, j):
                if j == 0:
                    need(dve, s_oev, q * 24)
                need(dve, s_fb, q * 8 + (j + 1 - 8))
                need(dve, s_fbr, q * 8 + (j - 8))
                dve.tensor_tensor(fbm[:, :, :], fb_bank[:, 0:NG * P].rearrange("p (g t) -> p g t", g=NG),
                                  o[:, par, :, j * P:(j + 1) * P], ALU.mult).then_inc(s_fbm, 1)
                need(dve, s_fbm, q * 8 + (j + 1 - 8))
                dve.tensor_reduce(o[:, par, 0, j * P:(j + 1) * P], fbm[:, :, :].rearrange("p g t -> p t g"),
                                  op=ALU.add, axis=AX_X).then_inc(s_fbr, 1)

            def body(it, k):
                m = Item(it, k)
                for t in range(9):
                    if m.attends and t < 8:
                        w0 = (1 - blocks_before(m.g, t)) * P
                        for h in range(2):
                            if h == 0:
                                need(dve, s_ptr, m.n(8, t))
                            need_apart(dve, s_scores, m.n(16, 2 * t + h + 1), s_apart)
                            c = m.g * 16 + h * 8 + t
                            mk = mask3[:, :] if m.g == 2 else mask[:, w0:]
                            dve.tensor_tensor_reduce(out=sp[:, h, w0:], in0=s_bank[h][:, w0:2 * P], in1=mk,
                                                     scale=1.0, scalar=3.0e38, op0=ALU.add, op1=ALU.min,
                                                     accum_out=st[:, c:c + 1]).then_inc(s_masked, 1)
                        if m.merges and m.g == 0 and t == 5:
                            differences(m.p())
                        if m.merges and m.g == 0 and t == 6:
                            factors(m.p())
                        if m.merges and m.g == 1:
                            merge_tile(m.p(), 1 - m.set, t)
                    if m.projects and 1 <= t <= 6:
                        s = t - 1
                        off, width = CHUNKS[s % 3]
                        need(dve, s_evac, m.n1(9, s + 1))
                        need_apart(dve, s_qp, m.n1(6, s), s_apart)
                        dve.stream_shuffle(rot[:, 0:width], ev[:, s % 2, 0:width], mask=swap).then_inc(s_shuf, 1)
                        need(dve, s_shuf, m.n1(6, s + 1))
                        dve.tensor_tensor(rot[:, 0:width], rot[:, 0:width], sin[:, off:off + width],
                                          ALU.mult).then_inc(s_t1, 1)
                    if m.projects and t in (1, 4, 7):
                        c1 = t // 3 + 1
                        if not (isinstance(it, int) and m.n1(3, c1) >= NB):
                            split_w(m.parity(3, c1), m.n1(3, c1 + 1))
                    if m.attends and t < 8:
                        c0 = (1 - blocks_before(m.g, t)) * 2 * P
                        need(dve, s_pthi, m.n(8, t + 1))
                        dve.tensor_tensor(pt_lo[:, c0:], pt_bank[:, c0:], f32(pt_hi[:, c0:]),
                                          ALU.subtract).then_inc(s_ptlo, 1)
            items(dve, body)
            differences(PAIRS)
            factors(PAIRS)
            for j in range(QT):
                merge_tile(PAIRS, (PAIRS - 1) % 2, j)

        @block.tensor
        def _(pe):
            def stats_transpose(q):
                need(pe, s_fbm, q * 8 + (-8))
                pe.transpose(fb_bank[0:96, 0:P], st[:, :], ident[:, :]).then_inc(s_sttr, 1)

            def spread_factors(q, j):
                if j == 0:
                    need(pe, s_f, q)
                need(pe, s_fbm, q * 8 + (j - 8))
                rhs = [x[:, :, :].rearrange("r g t -> r (g t)") for x in (f_hi, f_lo)]
                pe.matmul(fb_bank[:, 0:NG * P], sel[:, j, :], rhs[0], start=True, stop=False)
                pe.matmul(fb_bank[:, 0:NG * P], sel[:, j, :], rhs[1], start=False, stop=True).then_inc(s_fb, 1)

            def body(it, k):
                m = Item(it, k)
                for t in range(9):
                    if m.attends and t < 8:
                        if m.merges and m.g == 0 and t == 0:
                            need(pe, s_probs, m.n(16))
                            stats_transpose(m.p())
                        nb = blocks_before(m.g, t)
                        w0 = (1 - nb) * P
                        if t == 0:
                            need(pe, s_kqlo, m.n(6, 6))
                        if t == 0 and k == 0:
                            pe.wait_ge(s_const, 16 * 6)
                        need(pe, s_masked, m.n(16, 2 * t))
                        for h in range(2):
                            rows = slice(64 * h, 64 * h + 64)
                            q_cols, k_cols = slice(t * P, (t + 1) * P), slice((t - nb) * P, (t + 1) * P)
                            product(pe, s_bank[h][:, w0:2 * P],
                                    kq_hi[rows, m.buf, 1, q_cols], kq_lo[rows, m.buf, 1, q_cols],
                                    kq_hi[rows, m.buf, 0, k_cols], kq_lo[rows, m.buf, 0, k_cols],
                                    True, True).then_inc(s_scores, 1)
                        if t < 2:
                            need(pe, s_evac, m.n(9, 9))
                            need(pe, s_vev, m.n(2, t))
                            for i in range(4):
                                last = pe.transpose(v_bank[:, i * P:(i + 1) * P],
                                                    vt[:, (4 * t + i) * P:(4 * t + i + 1) * P], ident[:, :])
                            last.then_inc(s_vtr, 1)
                        if m.merges and m.g == 1:
                            spread_factors(m.p(), t)
                    if m.projects:
                        off, width = CHUNKS[t % 3]
                        if t % 3 == 0:
                            need(pe, s_wlo, m.n1(3, t // 3 + 1))
                        if k == -1 and t == 0:
                            pe.wait_ge(s_xlo, KT)
                        need(pe, s_evac, m.n1(9, t - 1))
                        par = m.parity(3, t // 3)
                        bank = gb[m.parity(9, t)]
                        for kt in range(KT):
                            last = product(pe, bank[:, 0:width], w_hi[:, par, kt, :], w_lo[:, par, kt, :],
                                           x_hi[:, kt, off:off + width], x_lo[:, kt, off:off + width],
                                           kt == 0, kt == KT - 1)
                        last.then_inc(s_gemm, 1)
                    if m.attends and t >= 1:
                        need(pe, s_ptlo, m.n(8, t))
                        need(pe, s_oev, m.n(8, t - 1))
                        if t in (1, 5):
                            need(pe, s_vlo, m.n(2, 1 + t // 5))
                        nb = blocks_before(m.g, t - 1)
                        for b in range(1 - nb, 2):
                            kt = t - 2 + b
                            cols = slice(b * 2 * P, (b + 1) * 2 * P)
                            last = product(pe, pv_bank[:, 0:2 * P], v_hi[:, kt, :], v_lo[:, kt, :],
                                           pt_hi[:, cols], pt_lo[:, cols], b == 1 - nb, b == 1)
                        last.then_inc(s_pv, 1)
                    if m.attends and t < 8:
                        need(pe, s_probs, m.n(16, 2 * t + 2))
                        need(pe, s_ptlo, m.n(8, t))
                        for b in range(1 - blocks_before(m.g, t), 2):
                            for h in range(2):
                                c = (2 * b + h) * P
                                last = pe.transpose(pt_bank[:, c:c + P], sp[:, h, b * P:(b + 1) * P], ident[:, :])
                        last.then_inc(s_ptr, 1)
            items(pe, body)
            stats_transpose(PAIRS)
            for j in range(QT):
                spread_factors(PAIRS, j)


class Lin:

    def __init__(self, c, it=0, per=0):
        self.c, self.it, self.per = c, it, per

    def plus(self, k):
        return Lin(self.c + k, self.it, self.per)

    def val(self, k=0):
        return self.c + k if self.per == 0 else self.it * self.per + (self.c + k)

    def div(self, d, k=0, scale=1):
        c = scale * (self.c // d + k)
        return c if self.per == 0 else self.it * (self.per // d * scale) + c

    def mod(self, d):
        return self.c % d


UP_BLOCKS = 2 * FT
DOWN_PIECES = (8, 8, 6)
FFN_BLOCKS = UP_BLOCKS + KT * len(DOWN_PIECES)
N_BLOCKS = NCH * (KT + FFN_BLOCKS)


def trunk(nc, x_hi, x_lo, dram, layer):
    ctx = ExitStack()
    sems = []
    final = layer == 1
    with ctx:
        def sb(name, shape, dt=F32):
            return ctx.enter_context(nc.sbuf_tensor(f"t{layer}_" + name, shape, dt))

        def sem(name):
            return semaphore(nc, f"t{layer}_" + name, sems)

        banks = [ctx.enter_context(nc.psum_tensor(f"t{layer}_bank{i}", [P, 512], F32)) for i in range(8)]
        g_bank, u_bank, z_bank, mean_bank, var_bank = banks[0:2], banks[2:4], banks[4:6], banks[6], banks[7]

        h_hi = sb("h_hi", [P, FT, CW], F32R)
        h_lo = sb("h_lo", [P, FT, CW], F32R)
        raw = sb("raw", [P, 4, KT * P])
        w_hi = sb("w_hi", [P, 2, KT * P], F32R)
        w_lo = sb("w_lo", [P, 2, KT * P], F32R)
        z = sb("z", [P, 2, KT, CW])
        zt = sb("zt", [P, 2, CW])
        sq = sb("sq", [P, 4, CW])
        sums = sb("sums", [P, CW])
        sums2 = sb("sums2", [P, 2, CW])
        rstd = sb("rstd", [P, CW])
        gbuf = sb("gbuf", [P, 2, CW + 2])
        acc = sb("acc", [P, 2, CW])
        hf = sb("hf", [P, 2, CW])
        hist = sb("hist", [P, FT, 2])
        gtail = sb("gtail", [P, FT, 2 + NS])
        state = sb("state", [P, FT, 2, NS])
        taps = sb("taps", [P, FT, 4])
        ln = sb("ln", [P, 2, 2, KT])
        bias = sb("bias", [P, KT])
        mean_w = sb("mean_w", [P, P])
        eps = sb("eps", [P, 1])

        s_apart = sem("apart")
        s_const, s_oin, s_ohi, s_olo, s_set = (sem(x) for x in ("const", "oin", "ohi", "olo", "set"))
        w_in = [sem(f"w_in{i}") for i in range(4)]
        s_whi, s_blk = sem("whi"), sem("blk")
        s_wlo = [sem("wlo_dve"), sem("wlo_pool")]
        s_ze, s_zx, s_z, s_add = (sem(x) for x in ("ze", "zx", "z", "add"))
        s_gev, s_hist, s_save, s_cv, s_conv, s_silu, s_mul, s_hhi, s_hlo = (
            sem(x) for x in ("gev", "hist", "save", "cv", "conv", "silu", "mul", "hhi", "hlo"))
        s_mean, s_zc, s_sq, s_red, s_var, s_sd, s_rstd, s_norm, s_xhi, s_y, s_ln, s_out = (
            sem(x) for x in ("mean", "zc", "sq", "red", "var", "sd", "rstd", "norm", "xhi", "y", "lnd", "out"))

        def stage_of(kind, c):
            return c if kind == "o" else NCH + c

        def walk(eng, slot, hook, done):
            for c in range(NCH):
                for m in range(KT):
                    if c > 0:
                        hook(c - 1, m)
                    slot("o", c, m, 0, Lin(KT * c + m))
            for c in range(NCH):
                base = NCH * KT + FFN_BLOCKS * c
                for m in range(4):
                    for j, kind in enumerate("gu"):
                        hook(NCH + c - 1, 2 * m + j)
                        slot(kind, c, m, j, Lin(base + 2 * m + j))
                with eng.Fori(2, FT // 2) as it:
                    for m in range(2):
                        for j, kind in enumerate("gu"):
                            slot(kind, c, it * 2 + m, j, Lin(base + 2 * m + j, it, 4))
                for m in range(KT):
                    for j in range(len(DOWN_PIECES)):
                        slot("d", c, m, j, Lin(base + UP_BLOCKS + 3 * m + j))
            done()
            for i in range(8):
                hook(2 * NCH - 1, i)

        def pieces_next(kind, j):
            return DOWN_PIECES[2] if kind == "d" and j == 1 else KT

        def unit(c, m, k=0):
            return m + (FT * c + k)

        def par(m):
            return m % 2 if isinstance(m, int) else m_parity[0]

        m_parity = [0]

        def z_index(kind, c, m):
            return KT * stage_of(kind, c) + m

        def before(kind, c, m):
            if kind == "o" and (c, m) != (0, 0):
                return ("o", c, m - 1) if m else ("o", c - 1, KT - 1)
            if kind == "g" and isinstance(m, int) and m == 0:
                return ("o", NCH - 1, KT - 1) if c == 0 else ("d", c - 1, KT - 1)
            if kind == "d" and m > 0:
                return ("d", c, m - 1)
            return None

        ctx.callback(clear, nc, sems)
        block = ctx.enter_context(nc.Block())

        @block.sync
        def _(sp):
            def source(kind, m, j):
                if kind == "o":
                    return dram["w_o"][m], KT
                if kind in "gu":
                    return take(dram["w_up"], m * 2 + j), KT
                return dram["w_down"][3 * m + j], DOWN_PIECES[j]

            def load_o(c):
                off, n = CHUNKS[c]
                need(sp, s_olo, 2 * c)
                for half, stage in enumerate((h_hi, h_lo)):
                    sp.dma_start(f32(stage[:, 16:20, 0:n]),
                                 dram["o_scr"].rearrange("(m p) t -> p m t", p=P)[:, 4 * half:4 * half + 4, off:off + n]
                                 ).then_inc(s_oin, 16)
                need(sp, s_oin, 32 * (c + 1))

            def slot(kind, c, m, j, b):
                if kind == "o" and m in (0, 5):
                    if c == 0 and m == 0:
                        load_o(0)
                    elif m == 5 and c + 1 < NCH:
                        load_o(c + 1)
                src, nk = source(kind, m, j)
                need(sp, s_wlo[b.mod(2)], b.div(2, -1))
                sp.dma_start(raw[:, b.mod(4), 0:nk * P], src[:, 0:nk * P]).then_inc(w_in[b.mod(4)], 16)
                if kind == "o" and c == 0 and m == 3:
                    for dst, name in ((state[:, :, :, :], "state"), (taps[:, :, :], "taps"),
                                      (ln[:, :, :, :], "ln"), (bias[:, :], "bias_o")):
                        sp.dma_start(dst, dram[name][layer]).then_inc(s_const, 16)

            def hook(l, i):
                if final and l >= NCH and i == 7:
                    store_y(l)

            def store_y(l):
                off, n = CHUNKS[l - NCH]
                need(sp, s_y, 8 * (l + 1))
                sp.dma_start(dram["yT"].rearrange("(m p) t -> p m t", p=P)[:, :, off:off + n],
                             z[:, l % 2, :, 0:n]).then_inc(s_out, 16)

            def done():
                need(sp, s_save, NCH * FT)
                sp.dma_start(dram["gT"][layer], gtail[:, :, :]).then_inc(s_out, 16)

            walk(sp, slot, hook, done)
            need(sp, s_out, 16 * (4 if final else 1))

        @block.scalar
        def _(act):
            def split(b, nk):
                act.wait_ge(w_in[b.mod(4)], b.div(4, 1, 16))
                need(act, s_blk, b.val(-1))
                act.copy(w_hi[:, b.mod(2), 0:nk * P], raw[:, b.mod(4), 0:nk * P]).then_inc(s_whi, 1)

            def split_o(c):
                n = CHUNKS[c][1]
                need(act, s_oin, 32 * (c + 1))
                for half, stage in enumerate((h_hi, h_lo)):
                    a = 8 * (c % 2) + 4 * half
                    act.copy(h_hi[:, a:a + 4, 0:n], f32(stage[:, 16:20, 0:n])).then_inc(s_ohi, 1)

            def evacuate_z(kind, c, m):
                zi, n = z_index(kind, c, m), CHUNKS[c][1]
                last = NCH * KT + FFN_BLOCKS * c + UP_BLOCKS + 3 * m + 3 if kind == "d" else KT * c + m + 1
                need(act, s_blk, last)
                need(act, s_zx, zi - 1)
                if kind == "o":
                    act.activation(zt[:, m % 2, 0:n], z_bank[m % 2][:, 0:n], ACT.Identity,
                                   bias=bias[:, m:m + 1]).then_inc(s_ze, 1)
                else:
                    act.copy(zt[:, m % 2, 0:n], z_bank[m % 2][:, 0:n]).then_inc(s_ze, 1)

            def silu(c, m, mp):
                n = CHUNKS[c][1]
                need(act, s_conv, unit(c, m, 1))
                act.activation(acc[:, mp, 0:n], acc[:, mp, 0:n], ACT.Silu).then_inc(s_silu, 1)

            def high_h(c, m, mp):
                n = CHUNKS[c][1]
                need(act, s_mul, unit(c, m, 1))
                dst = h_hi[:, m, 0:n] if isinstance(m, int) else \
                    h_hi[:, bass.ds(m, 1), 0:n].rearrange("p o t -> p (o t)")
                act.copy(dst, hf[:, mp, 0:n]).then_inc(s_hhi, 1)

            def slot(kind, c, m, j, b):
                n = CHUNKS[c][1]
                if kind == "o" and m == 0 and c == 0:
                    act.wait_ge(s_const, 64)
                    split(Lin(0), KT)
                    split_o(0)
                if not (b.per == 0 and b.c == N_BLOCKS - 1):
                    split(b.plus(1), pieces_next(kind, j))
                prev = before(kind, c, m) if j == 0 else None
                if prev:
                    evacuate_z(*prev)
                if kind == "o" and m == 6 and c + 1 < NCH:
                    split_o(c + 1)
                mp = b.c // 2 % 2
                if kind == "g" and not (isinstance(m, int) and m == 0):
                    silu(c, m - 1, 1 - mp)
                if kind == "u":
                    need(act, s_blk, b.val())
                    need(act, s_conv, unit(c, m, -1))
                    need(act, s_save, unit(c, m, -1))
                    act.copy(gbuf[:, mp, 2:2 + n], g_bank[mp][:, 0:n]).then_inc(s_gev, 1)
                    if not (isinstance(m, int) and m == 0):
                        high_h(c, m - 1, 1 - mp)
                if kind == "d" and m == 0 and j == 0:
                    silu(c, FT - 1, (FT - 1) % 2)
                if kind == "d" and m == 0 and j == 1:
                    high_h(c, FT - 1, (FT - 1) % 2)

            def hook(l, i):
                c, n, zp = l % NCH, CHUNKS[l % NCH][1], l % 2
                off = CHUNKS[c][0]
                if i in (2, 3):
                    half = i - 2
                    need(act, s_zc, l + 1)
                    need(act, s_red, 2 * l + half)
                    act.activation(sq[:, :, 0:n], z[:, zp, 4 * half:4 * half + 4, 0:n], ACT.Square).then_inc(s_sq, 1)
                if i == 4:
                    need(act, s_var, l + 1)
                    need(act, s_norm, l)
                    act.activation(rstd[:, 0:n], var_bank[:, 0:n], ACT.Sqrt, bias=eps[:, 0:1]).then_inc(s_sd, 1)
                if i == 5:
                    need(act, s_norm, l + 1)
                    for m in range(KT):
                        if final and l >= NCH:
                            act.activation(z[:, zp, m, 0:n], z[:, zp, m, 0:n], ACT.Identity,
                                           scale=ln[:, l // NCH, 0, m:m + 1],
                                           bias=ln[:, l // NCH, 1, m:m + 1]).then_inc(s_y, 1)
                        else:
                            act.activation(x_hi[:, m, off:off + n], z[:, zp, m, 0:n], ACT.Identity,
                                           scale=ln[:, l // NCH, 0, m:m + 1],
                                           bias=ln[:, l // NCH, 1, m:m + 1]).then_inc(s_xhi, 1)

            walk(act, slot, hook, lambda: evacuate_z("d", NCH - 1, KT - 1))

        @block.gpsimd
        def _(pool):
            pool.memset(hist[:, :, :], 0.0).then_inc(s_set, 1)
            pool.memset(mean_w[:, :], 1.0 / D).then_inc(s_set, 1)
            pool.memset(eps[:, :], LN_EPS).then_inc(s_set, 1)

            def split(b, nk):
                need(pool, s_whi, b.val(1))
                pool.tensor_tensor(w_lo[:, 1, 0:nk * P], raw[:, b.mod(4), 0:nk * P],
                                   f32(w_hi[:, 1, 0:nk * P]), ALU.subtract).then_inc(s_wlo[1], 1)

            def add_z(kind, c, m):
                if m == 0:
                    return
                zi, n, zp = z_index(kind, c, m), CHUNKS[c][1], stage_of(kind, c) % 2
                stage = stage_of(kind, c)
                need(pool, s_z, zi + 1)
                if m == 1:
                    need(pool, s_mean, stage)
                else:
                    need(pool, s_add, 7 * stage + m - 1)
                first = z[:, zp, 0, 0:n] if m == 1 else sums[:, 0:n]
                pool.tensor_tensor(sums[:, 0:n], first, z[:, zp, m, 0:n], ALU.add).then_inc(s_add, 1)

            def low_h(c, m, mp):
                n = CHUNKS[c][1]
                need(pool, s_hhi, unit(c, m, 1))
                hi, lo = ((x[:, m, 0:n] if isinstance(m, int) else
                           x[:, bass.ds(m, 1), 0:n].rearrange("p o t -> p (o t)")) for x in (h_hi, h_lo))
                pool.tensor_tensor(lo, hf[:, mp, 0:n], f32(hi), ALU.subtract).then_inc(s_hlo, 1)

            def row(ap, m):
                return ap[:, m, :] if isinstance(m, int) else ap[:, bass.ds(m, 1), :].rearrange("p o t -> p (o t)")

            def slot(kind, c, m, j, b):
                n = CHUNKS[c][1]
                mp = b.c // 2 % 2
                if b.mod(2) == 0 and not (b.per == 0 and b.c == N_BLOCKS - 1):
                    split(b.plus(1), pieces_next(kind, j))
                prev = before(kind, c, m) if j == 0 else None
                if prev:
                    add_z(*prev)
                if kind == "g":
                    if c == 0 and isinstance(m, int) and m == 0:
                        pool.wait_ge(s_set, 1)
                    if c > 0:
                        need(pool, s_save, unit(c, m, -FT + 1))
                    need_apart(pool, s_conv, unit(c, m, -1), s_apart)
                    pool.tensor_copy(gbuf[:, mp, 0:2], row(hist, m)).then_inc(s_hist, 1)
                if kind == "u":
                    need(pool, s_gev, unit(c, m, 1))
                    need_apart(pool, s_hist, unit(c, m, 1), s_apart)
                    if c < NCH - 1:
                        pool.tensor_copy(row(hist, m), gbuf[:, mp, n:n + 2]).then_inc(s_save, 1)
                    else:
                        pool.tensor_copy(row(gtail, m), gbuf[:, mp, n - NS:n + 2]).then_inc(s_save, 1)
                    if not (isinstance(m, int) and m == 0):
                        low_h(c, m - 1, 1 - mp)
                if kind == "d" and m == 0 and j == 1:
                    low_h(c, FT - 1, (FT - 1) % 2)

            def hook(l, i):
                n, zp = CHUNKS[l % NCH][1], l % 2
                if i == 6 and not (final and l >= NCH):
                    for m in range(KT):
                        need(pool, s_xhi, KT * l + m + 1)
                        pool.tensor_scalar(z[:, zp, m, 0:n], z[:, zp, m, 0:n], ln[:, l // NCH, 0, m:m + 1],
                                           ln[:, l // NCH, 1, m:m + 1], ALU.mult, ALU.add).then_inc(s_y, 1)

            walk(pool, slot, hook, lambda: add_z("d", NCH - 1, KT - 1))

        @block.vector
        def _(dve):
            def split(b, nk):
                need(dve, s_whi, b.val(1))
                dve.tensor_tensor(w_lo[:, 0, 0:nk * P], raw[:, b.mod(4), 0:nk * P],
                                  f32(w_hi[:, 0, 0:nk * P]), ALU.subtract).then_inc(s_wlo[0], 1)

            def split_o(c):
                n = CHUNKS[c][1]
                for half, stage in enumerate((h_hi, h_lo)):
                    a = 8 * (c % 2) + 4 * half
                    need(dve, s_ohi, 2 * c + half + 1)
                    dve.tensor_tensor(h_lo[:, a:a + 4, 0:n], f32(stage[:, 16:20, 0:n]), f32(h_hi[:, a:a + 4, 0:n]),
                                      ALU.subtract).then_inc(s_olo, 1)

            def residual(kind, c, m):
                zi, (off, n) = z_index(kind, c, m), CHUNKS[c]
                stage = stage_of(kind, c)
                dst = z[:, stage % 2, m, 0:n]
                if m == 0:
                    if final and stage >= NCH + 2:
                        need(dve, s_out, 16 * (stage - NCH - 1))
                    else:
                        need(dve, s_ln, stage - 1)
                need(dve, s_ze, zi + 1)
                dve.scalar_tensor_tensor(out=dst, in0=f32(x_hi[:, m, off:off + n]), scalar=ALPHA,
                                         in1=zt[:, m % 2, 0:n], op0=ALU.mult, op1=ALU.add).then_inc(s_zx, 1)
                need(dve, s_zx, zi + 1)
                dve.scalar_tensor_tensor(out=dst, in0=f32(x_lo[:, m, off:off + n]), scalar=ALPHA,
                                         in1=dst, op0=ALU.mult, op1=ALU.add).then_inc(s_z, 1)

            def tap(m, i):
                return taps[:, m, i:i + 1] if isinstance(m, int) else \
                    taps[:, bass.ds(m, 1), i:i + 1].rearrange("p o t -> p (o t)")

            def chain(c, m, i, ins):
                steps = 2 if c < NCH - 1 else 3
                ins.then_inc(s_cv, 1)
                need(dve, s_cv, m * steps + (2 * FT * c + i + 1))

            def convolve(c, m, mp):
                n = CHUNKS[c][1]
                k = n if c < NCH - 1 else n - NS
                a = acc[:, mp, 0:k]
                need(dve, s_gev, unit(c, m, 1))
                need(dve, s_hist, unit(c, m, 1))
                need(dve, s_mul, unit(c, m, -1))
                ins = dve.tensor_scalar(a, gbuf[:, mp, 0:k], tap(m, 0), tap(m, 3), ALU.mult, ALU.add)
                if c == NCH - 1:
                    s = acc[:, mp, k:n]
                    st = (lambda i: state[:, m, i, :]) if isinstance(m, int) else (
                        lambda i: state[:, bass.ds(m, 1), i, :].rearrange("p o t -> p (o t)"))
                    ins = dve.tensor_scalar(s, st(0), tap(m, 0), tap(m, 3), ALU.mult, ALU.add)
                    chain(c, m, 0, ins)
                    ins = dve.scalar_tensor_tensor(out=s, in0=st(1), scalar=tap(m, 1), in1=s,
                                                   op0=ALU.mult, op1=ALU.add)
                    chain(c, m, 1, ins)
                    dve.scalar_tensor_tensor(out=a, in0=gbuf[:, mp, 1:1 + k], scalar=tap(m, 1), in1=a,
                                             op0=ALU.mult, op1=ALU.add)
                    ins = dve.scalar_tensor_tensor(out=s, in0=gbuf[:, mp, 2 + k:2 + n], scalar=tap(m, 2), in1=s,
                                                   op0=ALU.mult, op1=ALU.add)
                    chain(c, m, 2, ins)
                    dve.scalar_tensor_tensor(out=a, in0=gbuf[:, mp, 2:2 + k], scalar=tap(m, 2), in1=a,
                                             op0=ALU.mult, op1=ALU.add).then_inc(s_conv, 1)
                else:
                    chain(c, m, 0, ins)
                    ins = dve.scalar_tensor_tensor(out=a, in0=gbuf[:, mp, 1:1 + k], scalar=tap(m, 1), in1=a,
                                                   op0=ALU.mult, op1=ALU.add)
                    chain(c, m, 1, ins)
                    dve.scalar_tensor_tensor(out=a, in0=gbuf[:, mp, 2:2 + k], scalar=tap(m, 2), in1=a,
                                             op0=ALU.mult, op1=ALU.add).then_inc(s_conv, 1)

            def gate(c, m, mp, b_done):
                n = CHUNKS[c][1]
                need(dve, s_blk, b_done)
                need(dve, s_silu, unit(c, m, 1))
                need(dve, s_hlo, unit(c, m, -1))
                dve.tensor_tensor(hf[:, mp, 0:n], acc[:, mp, 0:n], u_bank[mp][:, 0:n], ALU.mult).then_inc(s_mul, 1)

            def slot(kind, c, m, j, b):
                mp = b.c // 2 % 2
                if kind == "o" and m == 0 and c == 0:
                    dve.wait_ge(s_const, 64)
                    split(Lin(0), KT)
                    split_o(0)
                if b.mod(2) == 1 and not (b.per == 0 and b.c == N_BLOCKS - 1):
                    split(b.plus(1), pieces_next(kind, j))
                prev = before(kind, c, m) if j == 0 else None
                if prev:
                    residual(*prev)
                if kind == "o" and m == 6 and c + 1 < NCH:
                    split_o(c + 1)
                if kind == "g" and not (isinstance(m, int) and m == 0):
                    gate(c, m - 1, 1 - mp, b.val())
                if kind == "u":
                    convolve(c, m, mp)
                if kind == "d" and m == 0 and j == 0:
                    gate(c, FT - 1, (FT - 1) % 2, b.val())

            def hook(l, i):
                c, n, zp = l % NCH, CHUNKS[l % NCH][1], l % 2
                off = CHUNKS[c][0]
                zz = z[:, zp, :, 0:n]
                if i == 1:
                    need(dve, s_mean, l + 1)
                    mean = mean_bank[:, 0:n].unsqueeze(1).broadcast_to((P, KT, n))
                    dve.tensor_tensor(zz, zz, mean, ALU.subtract).then_inc(s_zc, 1)
                if i in (2, 3):
                    half = i - 2
                    need(dve, s_sq, 2 * l + half + 1)
                    need(dve, s_var, l)
                    dve.tensor_reduce(sums2[:, half, 0:n], sq[:, :, 0:n].rearrange("p m t -> p t m"),
                                      op=ALU.add, axis=AX_X).then_inc(s_red, 1)
                if i == 4:
                    need(dve, s_sd, l + 1)
                    dve.reciprocal(rstd[:, 0:n], rstd[:, 0:n]).then_inc(s_rstd, 1)
                    need(dve, s_rstd, l + 1)
                    dve.tensor_tensor(zz, zz, rstd[:, 0:n].unsqueeze(1).broadcast_to((P, KT, n)),
                                      ALU.mult).then_inc(s_norm, 1)
                if i == 7 and not (final and l >= NCH):
                    need(dve, s_y, KT * (l + 1))
                    dve.tensor_tensor(x_lo[:, :, off:off + n], zz, f32(x_hi[:, :, off:off + n]),
                                      ALU.subtract).then_inc(s_ln, 1)

            walk(dve, slot, hook, lambda: residual("d", NCH - 1, KT - 1))

        @block.tensor
        def _(pe):
            def slot(kind, c, m, j, b):
                off, n = CHUNKS[c]
                mp = b.c // 2 % 2
                need(pe, s_wlo[b.mod(2)], b.div(2, 1))
                wp = b.mod(2)
                first, last_block, nk, k0 = True, True, KT, 0
                if kind == "o":
                    if m == 0:
                        need(pe, s_olo, 2 * (c + 1))
                    need(pe, s_ze, z_index(kind, c, m) - 1)
                    out = z_bank[m % 2]
                    xh, xl = ((lambda kt, x=x: x[:, 8 * (c % 2) + kt, 0:n]) for x in (h_hi, h_lo))
                elif kind in "gu":
                    if isinstance(m, int) and m == 0 and j == 0:
                        need(pe, s_ln, c + 1)
                    if kind == "g":
                        need(pe, s_gev, unit(c, m, -1))
                        out = g_bank[mp]
                    else:
                        need(pe, s_mul, unit(c, m, -1))
                        out = u_bank[mp]
                    xh, xl = ((lambda kt, x=x: x[:, kt, off:off + n]) for x in (x_hi, x_lo))
                else:
                    nk, k0 = DOWN_PIECES[j], 8 * j
                    first, last_block = j == 0, j == 2
                    if m == 0:
                        need(pe, s_hlo, FT * c + k0 + nk)
                    if j == 0:
                        need(pe, s_ze, z_index(kind, c, m) - 1)
                    out = z_bank[m % 2]
                    xh, xl = ((lambda kt, x=x: x[:, k0 + kt, 0:n]) for x in (h_hi, h_lo))
                for kt in range(nk):
                    cols = slice(kt * P, (kt + 1) * P)
                    last = product(pe, out[:, 0:n], w_hi[:, wp, cols], w_lo[:, wp, cols], xh(kt), xl(kt),
                                   first and kt == 0, last_block and kt == nk - 1)
                last.then_inc(s_blk, 1)

            def hook(l, i):
                n = CHUNKS[l % NCH][1]
                if i == 1:
                    if l == 0:
                        pe.wait_ge(s_set, 3)
                    need(pe, s_add, 7 * (l + 1))
                    need(pe, s_zc, l)
                    pe.matmul(mean_bank[:, 0:n], mean_w[:, :], sums[:, 0:n], start=True, stop=True).then_inc(s_mean, 1)
                if i == 4:
                    need(pe, s_red, 2 * (l + 1))
                    need(pe, s_sd, l)
                    pe.matmul(var_bank[:, 0:n], mean_w[:, :], sums2[:, 0, 0:n], start=True, stop=False)
                    pe.matmul(var_bank[:, 0:n], mean_w[:, :], sums2[:, 1, 0:n], start=False, stop=True
                              ).then_inc(s_var, 1)

            walk(pe, slot, hook, lambda: None)


def mixer_b(nc, x_hi, x_lo, dram):
    ctx = ExitStack()
    sems = []
    with ctx:
        def sb(name, shape, dt=F32):
            return ctx.enter_context(nc.sbuf_tensor("b_" + name, shape, dt))

        def ps(name):
            return ctx.enter_context(nc.psum_tensor("b_" + name, [P, 512], F32))

        def sem(name):
            return semaphore(nc, "b_" + name, sems)

        raw = sb("raw", [P, 2, KT * P])
        w_hi = sb("w_hi", [P, 2, KT * P], F32R)
        w_lo = sb("w_lo", [P, 2, KT * P], F32R)
        k_hi = sb("k_hi", [P, NKV_B, SEQ], F32R)
        k_lo = sb("k_lo", [P, NKV_B, SEQ], F32R)
        q_hi = sb("q_hi", [P, 2, SEQ], F32R)
        q_lo = sb("q_lo", [P, 2, SEQ], F32R)
        v_hi = sb("v_hi", [P, NKV_B, QT, 2, HD], F32R)
        v_lo = sb("v_lo", [P, NKV_B, QT, 2, HD], F32R)
        vt = sb("vt", [P, T])
        vraw = sb("vraw", [P, 4, NKV_B, HD])
        cos = sb("cos", [P, T])
        sin = sb("sin", [P, T])
        mask = sb("mask", [P, 2 * P])
        ident = sb("ident", [P, P])
        ev = sb("ev", [P, 2, CW])
        rot = sb("rot", [P, CW])
        t2 = sb("t2", [P, CW])
        qp = sb("qp", [P, 2, CW])
        sp = sb("sp", [P, 2, 2, 2 * P])
        pt_hi = sb("pt_hi", [P, 4 * P], F32R)
        pt_lo = sb("pt_lo", [P, 4 * P], F32R)
        o = sb("o", [P, 2, SEQ])
        nm0 = sb("nm0", [P, 2, 2])
        nm = sb("nm", [P, 2, 2])
        ts = sb("ts", [P, 2, 2])
        es = sb("es", [P, 2, 2])
        den = sb("den", [P, 2, 2])
        rden = sb("rden", [P, 2, 2])
        nsink = sb("nsink", [P, NH])
        bias = sb("bias", [P, 3 + PAIRS])

        gb = [ps(f"gemm{i}") for i in range(2)]
        s_bank = [[ps(f"scores{i}{h}") for h in range(2)] for i in range(2)]
        pt_bank = ps("probsT")
        pv_bank = ps("pv")

        s_const, s_prep = sem("const"), sem("prep")
        w_in = [sem("w_in0"), sem("w_in1")]
        s_whi, s_wlo, s_gemm, s_evac = (sem(x) for x in ("whi", "wlo", "gemm", "evac"))
        s_shuf, s_t1, s_t2, s_qp, s_rhi, s_rlo = (sem(x) for x in ("shuf", "t1", "t2", "qp", "rhi", "rlo"))
        r_out = [sem("r_out0"), sem("r_out1")]
        s_vout, s_vtr, s_vev, s_vhi, s_vlo = (sem(x) for x in ("vout", "vtr", "vev", "vhi", "vlo"))
        (s_scores, s_masked, s_min, s_shift, s_probs, s_es, s_den, s_rden, s_normed, s_ptr, s_pthi, s_ptlo, s_pv,
         s_oev) = (sem(x) for x in ("scores", "masked", "min", "shift", "probs", "es", "den", "rden",
                                            "normed", "ptr", "pthi", "ptlo", "pv", "oev"))

        o_out = [sem("o_out0"), sem("o_out1")]

        NBLK = 3 + PAIRS
        NT = PAIRS * QT

        def chunk_of(r):
            return r if r < 6 else r + 3

        def stores(r):
            return r < 6 or r % 3 == 2

        def stores_before(r):
            return sum(stores(x) for x in range(r % 2, r, 2))

        def schedule(start, work, tail):
            start()
            for u in range(-1, NT + 1):
                n, t = divmod(u, QT)
                nxt = n + 1
                step = {1: 0, 3: 1, 5: 2}.get(t)
                mk = step if n >= 0 and nxt < PAIRS and step is not None else None
                rt = {2: 0, 4: 1, 6: 2}.get(t)
                rk = rt if n >= 0 and nxt < PAIRS and rt is not None else None
                work(u, nxt, mk, rk)
            tail()

        ctx.callback(clear, nc, sems)
        block = ctx.enter_context(nc.Block())

        @block.sync
        def _(sp_e):
            def load(b):
                need(sp_e, s_wlo, b - 1)
                sp_e.dma_start(raw[:, b % 2], dram["w_b"][b]).then_inc(w_in[b % 2], 16)

            def store(r):
                off, width = CHUNKS[r % 3]
                need(sp_e, s_qp, r + 1)
                if r < 6:
                    rows = slice(HD * (r // 3), HD * (r // 3) + HD)
                    sp_e.dma_start(dram["kT_b"][rows, off:off + width], qp[0:HD, r % 2, 0:width]
                                   ).then_inc(r_out[r % 2], 16)
                elif r % 3 == 2:
                    n = r // 3 - 2
                    sp_e.dma_start(dram["q_sb"][n * P:(n + 1) * P, :], qp[:, r % 2, width - NS:width]
                                   ).then_inc(r_out[r % 2], 16)

            def start():
                load(0)
                load(1)
                for dst, name in ((cos, "cos"), (sin, "sin"), (mask, "mask_b"), (ident, "ident"), (bias, "bias_b")):
                    sp_e.dma_start(dst[:, :], dram[name]).then_inc(s_const, 16)
                sp_e.dma_start(nsink[:, :], dram["sinks"].partition_broadcast(P)).then_inc(s_const, 16)
                load(2)
                for r in range(3):
                    store(r)
                load(3)
                for r in range(3, 6):
                    store(r)
                need(sp_e, s_evac, 9)
                sp_e.dma_start(dram["vT_b"], vt[:, :]).then_inc(s_vout, 16)
                load(4)
                for r in range(6, 9):
                    store(r)

            def work(u, nxt, mk, rk):
                n, t = divmod(u, QT)
                if t == 0 and nxt + 4 < NBLK:
                    load(nxt + 4)
                if rk is not None:
                    store(6 + 3 * nxt + rk)
                if t == 2 and n >= 1:
                    store_o(n - 1)

            def store_o(n):
                need(sp_e, s_oev, 8 * (n + 1))
                sp_e.dma_start(dram["o_scr"][n * P:(n + 1) * P, 0:SEQ], o[:, n % 2, :]).then_inc(o_out[n % 2], 16)

            def tail():
                store_o(PAIRS - 1)
                sp_e.wait_ge(s_vout, 16)
                for i in range(2):
                    sp_e.wait_ge(o_out[i], 16 * PAIRS // 2)
                    sp_e.wait_ge(r_out[i], 16 * sum(stores(x) for x in range(i, 6 + 3 * PAIRS, 2)))
            schedule(start, work, tail)

        @block.scalar
        def _(act):
            def split(b):
                act.wait_ge(w_in[b % 2], 16 * (b // 2 + 1))
                need(act, s_gemm, 3 * (b - 1))
                act.copy(w_hi[:, b % 2], raw[:, b % 2]).then_inc(s_whi, 1)

            def evacuate(c):
                b, ch = divmod(c, 3)
                off, width = CHUNKS[ch]
                need(act, s_gemm, c + 1)
                if b == 2:
                    act.activation(vt[:, off:off + width], gb[c % 2][:, 0:width], ACT.Identity,
                                   bias=bias[:, 2:3]).then_inc(s_evac, 1)
                    return
                r = c if b < 2 else c - 3
                need(act, s_qp, r - 1)
                act.activation(ev[:, r % 2, 0:width], gb[c % 2][:, 0:width], ACT.Identity, bias=bias[:, b:b + 1],
                               scale=1.0 if b < 2 else -SCALE).then_inc(s_evac, 1)

            def high(r):
                off, width = CHUNKS[r % 3]
                n = min(width, SEQ - off)
                dst = k_hi[:, r // 3, off:off + n] if r < 6 else q_hi[:, r // 3 % 2, off:off + n]
                need(act, s_qp, r + 1)
                act.copy(dst, qp[:, r % 2, 0:n]).then_inc(s_rhi, 1)

            def start():
                split(0)
                act.wait_ge(s_prep, 1)
                for b in range(3):
                    split(b + 1)
                    for ch in range(3):
                        evacuate(3 * b + ch)
                        if b < 2:
                            high(3 * b + ch)
                split(4)
                for u in range(2):
                    need(act, s_vtr, u + 1)
                    need(act, s_vlo, 2 * u)
                    act.copy(vraw[:, :, :, :].rearrange("p a b c -> p (a b c)"), pv_bank[:, :]).then_inc(s_vev, 1)
                for ch in range(3):
                    evacuate(9 + ch)
                    high(6 + ch)

            def work(u, nxt, mk, rk):
                n, t = divmod(u, QT)
                if 0 <= u < NT:
                    w0 = (1 - (t > 0)) * P
                    for h in range(2):
                        need(act, s_min, u + 1)
                        act.activation(sp[:, u % 2, h, w0:], sp[:, u % 2, h, w0:], ACT.Exp,
                                       bias=nm[:, u % 2, h:h + 1], scale=-1.0,
                                       accum_out=den[:, u % 2, h:h + 1]).then_inc(s_probs, 1)
                    need(act, s_shift, u + 1)
                    act.activation(es[:, u % 2, :], ts[:, u % 2, :], ACT.Exp).then_inc(s_es, 1)
                if rk is not None:
                    high(6 + 3 * nxt + rk)
                if mk == 1 and nxt + 4 < NBLK:
                    split(nxt + 4)
                if mk is not None:
                    evacuate(9 + 3 * nxt + mk)
                if u >= 1:
                    n1, t1 = divmod(u - 1, QT)
                    need(act, s_pv, u)
                    if t1 == 0:
                        need(act, o_out[n1 % 2], 16 * (n1 // 2))
                    for h in range(2):
                        rows = slice(64 * h, 64 * h + 64)
                        last = act.copy(o[rows, n1 % 2, t1 * P:(t1 + 1) * P], pv_bank[rows, h * P:(h + 1) * P])
                    last.then_inc(s_oev, 1)
                if 0 <= u < NT:
                    c0 = (1 - (t > 0)) * 2 * P
                    need(act, s_ptr, u + 1)
                    act.copy(pt_hi[:, c0:], pt_bank[:, c0:]).then_inc(s_pthi, 1)
            schedule(start, work, lambda: None)

        @block.gpsimd
        def _(pool):
            def rotate(r):
                c = chunk_of(r)
                off, width = CHUNKS[r % 3]
                n = min(width, SEQ - off)
                need(pool, s_evac, c + 1)
                pool.tensor_tensor(t2[:, 0:width], ev[:, r % 2, 0:width], cos[:, off:off + width],
                                   ALU.mult).then_inc(s_t2, 1)
                need(pool, s_t1, r + 1)
                need(pool, s_t2, r + 1)
                need(pool, s_rhi, r - 1)
                need(pool, r_out[r % 2], 16 * stores_before(r))
                pool.tensor_tensor(qp[:, r % 2, 0:width], rot[:, 0:width], t2[:, 0:width], ALU.add).then_inc(s_qp, 1)
                need(pool, s_rhi, r + 1)
                need(pool, s_qp, r + 1)
                hi, lo = (k_hi[:, r // 3], k_lo[:, r // 3]) if r < 6 else (q_hi[:, r // 3 % 2], q_lo[:, r // 3 % 2])
                pool.tensor_tensor(lo[:, off:off + n], qp[:, r % 2, 0:n], f32(hi[:, off:off + n]),
                                   ALU.subtract).then_inc(s_rlo, 1)

            def start():
                pool.wait_ge(s_const, 16 * 6)
                for r in range(6):
                    rotate(r)
                for u in range(2):
                    need(pool, s_vev, u + 1)
                    for kv in range(NKV_B):
                        src = vraw[:, :, kv, :].unsqueeze(2).broadcast_to((P, 4, 2, HD))
                        hi, lo = v_hi[:, kv, 4 * u:4 * u + 4], v_lo[:, kv, 4 * u:4 * u + 4]
                        pool.tensor_copy(hi, src).then_inc(s_vhi, 1)
                        need(pool, s_vhi, 2 * u + kv + 1)
                        pool.tensor_tensor(lo, src, f32(hi), ALU.subtract).then_inc(s_vlo, 1)
                for r in range(6, 9):
                    rotate(r)

            def work(u, nxt, mk, rk):
                if rk is not None:
                    rotate(6 + 3 * nxt + rk)
            schedule(start, work, lambda: None)

        @block.vector
        def _(dve):
            swap = [i ^ (ROT // 2) if i < ROT else i for i in range(32)]

            def split(b):
                need(dve, s_whi, b + 1)
                dve.tensor_tensor(w_lo[:, b % 2], raw[:, b % 2], f32(w_hi[:, b % 2]), ALU.subtract).then_inc(s_wlo, 1)

            def rotate(r):
                c = chunk_of(r)
                off, width = CHUNKS[r % 3]
                need(dve, s_evac, c + 1)
                need(dve, s_qp, r)
                dve.stream_shuffle(rot[:, 0:width], ev[:, r % 2, 0:width], mask=swap).then_inc(s_shuf, 1)
                need(dve, s_shuf, r + 1)
                dve.tensor_tensor(rot[:, 0:width], rot[:, 0:width], sin[:, off:off + width], ALU.mult).then_inc(s_t1, 1)

            def start():
                dve.wait_ge(s_const, 16 * 6)
                dve.tensor_scalar(nsink[:, :], nsink[:, :], -1.0, None, ALU.mult)
                dve.tensor_scalar(bias[:, 3:], bias[:, 3:], -SCALE, None, ALU.mult).then_inc(s_prep, 1)
                split(0)
                for b in range(3):
                    split(b + 1)
                    for ch in range(3):
                        if b < 2:
                            rotate(3 * b + ch)
                split(4)
                for r in range(6, 9):
                    rotate(r)

            def mask_scores(u):
                n, t = divmod(u, QT)
                w0 = (1 - (t > 0)) * P
                for h in range(2):
                    need(dve, s_scores, 2 * u + h + 1)
                    if h == 0:
                        need(dve, s_ptr, u - 1)
                    dve.tensor_tensor_reduce(out=sp[:, u % 2, h, w0:], in0=s_bank[u % 2][h][:, w0:2 * P],
                                             in1=mask[:, w0:], scale=1.0, scalar=3.0e38, op0=ALU.add, op1=ALU.min,
                                             accum_out=nm0[:, u % 2, h:h + 1]).then_inc(s_masked, 1)
                need(dve, s_masked, 2 * u + 2)
                sink = nsink[:, 2 * n:2 * n + 2]
                dve.tensor_tensor(nm[:, u % 2, :], nm0[:, u % 2, :], sink, ALU.min).then_inc(s_min, 1)
                need(dve, s_min, u + 1)
                dve.tensor_tensor(ts[:, u % 2, :], nm[:, u % 2, :], sink, ALU.subtract).then_inc(s_shift, 1)

            def normalise(u):
                n, t = divmod(u, QT)
                w0 = (1 - (t > 0)) * P
                need(dve, s_probs, 2 * u + 2)
                need(dve, s_es, u + 1)
                dve.tensor_tensor(den[:, u % 2, :], den[:, u % 2, :], es[:, u % 2, :], ALU.add).then_inc(s_den, 1)
                need(dve, s_den, u + 1)
                dve.reciprocal(rden[:, u % 2, :], den[:, u % 2, :]).then_inc(s_rden, 1)
                need(dve, s_rden, u + 1)
                for h in range(2):
                    dve.tensor_scalar(sp[:, u % 2, h, w0:], sp[:, u % 2, h, w0:], rden[:, u % 2, h:h + 1], None,
                                      ALU.mult).then_inc(s_normed, 1)

            def work(u, nxt, mk, rk):
                if u + 1 < NT:
                    mask_scores(u + 1)
                if 0 <= u < NT:
                    normalise(u)
                if rk is not None:
                    rotate(6 + 3 * nxt + rk)
                if mk == 1 and nxt + 4 < NBLK:
                    split(nxt + 4)
                if 0 <= u < NT:
                    c0 = (1 - (u % QT > 0)) * 2 * P
                    need(dve, s_pthi, u + 1)
                    dve.tensor_tensor(pt_lo[:, c0:], pt_bank[:, c0:], f32(pt_hi[:, c0:]), ALU.subtract
                                      ).then_inc(s_ptlo, 1)
            schedule(start, work, lambda: None)

        @block.tensor
        def _(pe):
            def chunk(c):
                b, ch = divmod(c, 3)
                off, width = CHUNKS[ch]
                if ch == 0:
                    need(pe, s_wlo, b + 1)
                need(pe, s_evac, c - 1)
                for kt in range(KT):
                    cols = slice(kt * P, (kt + 1) * P)
                    last = product(pe, gb[c % 2][:, 0:width], w_hi[:, b % 2, cols], w_lo[:, b % 2, cols],
                                   x_hi[:, kt, off:off + width], x_lo[:, kt, off:off + width], kt == 0, kt == KT - 1)
                last.then_inc(s_gemm, 1)

            def start():
                for c in range(9):
                    chunk(c)
                pe.wait_ge(s_const, 16 * 6)
                for u in range(2):
                    need(pe, s_evac, 9)
                    need(pe, s_vev, u)
                    for i in range(4):
                        j = 4 * u + i
                        last = pe.transpose(pv_bank[:, i * P:(i + 1) * P], vt[:, j * P:(j + 1) * P], ident[:, :])
                    last.then_inc(s_vtr, 1)
                for c in range(9, 12):
                    chunk(c)

            def scores(u):
                n, t = divmod(u, QT)
                nb = 1 if t > 0 else 0
                w0 = (1 - nb) * P
                if t == 0:
                    need(pe, s_rlo, 6 + 3 * (n + 1))
                need(pe, s_masked, 2 * (u - 1))
                for h in range(2):
                    rows = slice(64 * h, 64 * h + 64)
                    qc, kc = slice(t * P, (t + 1) * P), slice((t - nb) * P, (t + 1) * P)
                    kv = 2 * n // GQA_B
                    product(pe, s_bank[u % 2][h][:, w0:2 * P], q_hi[rows, n % 2, qc], q_lo[rows, n % 2, qc],
                            k_hi[rows, kv, kc], k_lo[rows, kv, kc], True, True).then_inc(s_scores, 1)

            def work(u, nxt, mk, rk):
                n, t = divmod(u, QT)
                if u + 1 < NT:
                    scores(u + 1)
                if mk is not None:
                    chunk(9 + 3 * nxt + mk)
                if u >= 1:
                    n1, t1 = divmod(u - 1, QT)
                    need(pe, s_ptlo, u)
                    need(pe, s_oev, u - 1)
                    if u == 1:
                        need(pe, s_vlo, 4)
                    nb, kv = (1 if t1 > 0 else 0), 2 * n1 // GQA_B
                    for b in range(1 - nb, 2):
                        kt = t1 - 1 + b
                        cols = slice(b * 2 * P, (b + 1) * 2 * P)
                        last = product(pe, pv_bank[:, 0:2 * P], v_hi[:, kv, kt].rearrange("p x d -> p (x d)"),
                                       v_lo[:, kv, kt].rearrange("p x d -> p (x d)"),
                                       pt_hi[:, cols], pt_lo[:, cols], b == 1 - nb, b == 1)
                    last.then_inc(s_pv, 1)
                if 0 <= u < NT:
                    need(pe, s_normed, 2 * u + 2)
                    need(pe, s_ptlo, u)
                    for b in range(1 - (t > 0), 2):
                        for h in range(2):
                            c = (2 * b + h) * P
                            last = pe.transpose(pt_bank[:, c:c + P], sp[:, u % 2, h, b * P:(b + 1) * P], ident[:, :])
                    last.then_inc(s_ptr, 1)
            schedule(start, work, lambda: None)


def decode(nc, dram, layer):
    ctx = ExitStack()
    sems = []
    ng = NG if layer == 0 else 1
    kc = KEYS + 1
    with ctx:
        def sb(name, shape, dt=F32):
            return ctx.enter_context(nc.sbuf_tensor(f"d{layer}_" + name, shape, dt))

        def sem(name):
            return semaphore(nc, f"d{layer}_" + name, sems)

        banks = [ctx.enter_context(nc.psum_tensor(f"d{layer}_bank{i}", [P, 512], F32)) for i in range(8)]
        RING = 6
        kp = KT if layer == 0 else 1
        vw = D if layer == 0 else P
        kb = sb("kb", [P, RING, kp, kc])
        vb = sb("vb", [P, RING, vw])
        qbd = sb("qbd", [P, ng, NS, kp, 32])
        qs = sb("qs", [P, ng, PAIRS, NS])
        ks = sb("ks", [P, ng, kp, NS])
        vs = sb("vs", [P, ng, PAIRS if layer == 0 else NKV_B, NS])
        probs = sb("probs", [P, 2, ng * kc])
        nmx = sb("nmx", [P, 2])
        den = sb("den", [P, 2])
        ts = sb("ts", [P, 2])
        es = sb("es", [P, 2])
        sink = sb("sink", [P, 1])
        pts = sb("pts", [P, 2, ng, P])
        diag = sb("diag", [P, vw])
        om = sb("om", [P, 2, vw])
        ident = sb("ident", [P, P])
        sel_b = sb("sel_b", [P, 4])
        sel_h = sb("sel_h", [P, P])
        own = sb("own", [P, PAIRS, 4])
        own_x = sb("own_x", [P, 2, PAIRS, 4])
        dn = sb("dn", [P, 2, ng, PAIRS, 4])
        pn = sb("pn", [P, ng, PAIRS, NS])
        om2 = sb("om2", [P, 2, HD])
        ot = sb("ot", [P, PAIRS, NS])
        ot2 = sb("ot2", [P, PAIRS, NS])

        s_in, s_k, s_v, s_kn, s_z, s_qbd, s_sc, s_vfree = (
            sem(x) for x in ("in", "k", "v", "kn", "z", "qbd", "sc", "vfree"))
        k_in = [sem(f"k_in{i}") for i in range(RING)]
        v_in = [sem(f"v_in{i}") for i in range(RING)]
        s_min, s_new, s_exp, s_es, s_norm, s_tr, s_pts, s_pv, s_om, s_dn, s_fin, s_ot, s_out = (
            sem(x) for x in ("min", "new", "exp", "es", "norm", "tr", "pts", "pv", "om", "dn", "fin", "ot", "out"))
        units = [(g, b) for g in range(ng) for b in range(NS)]
        vunits = [(g, b) for b in range(NS) for g in range(ng)]
        n_in = 6 + (3 * ng if layer == 0 else 8)

        ctx.callback(clear, nc, sems)
        block = ctx.enter_context(nc.Block())

        @block.sync
        def _(sp):
            if layer == 0:
                for g in range(ng):
                    sp.dma_start(qs[:, g], dram["q_s"][g].rearrange("(m p) s -> p m s", p=P)).then_inc(s_in, 16)
                    sp.dma_start(ks[:, g], dram["kT"][g].rearrange("(m p) s -> p m s", p=P)[:, :, SEQ:T]
                                 ).then_inc(s_in, 16)
                    sp.dma_start(vs[:, g], dram["vT"][g].rearrange("(m p) s -> p m s", p=P)[:, :, SEQ:T]
                                 ).then_inc(s_in, 16)
            else:
                for kv in range(NKV_B):
                    rows = slice(HD * kv, HD * kv + HD)
                    heads = dram["q_sb"][kv * GQA_B * HD:(kv + 1) * GQA_B * HD, :]
                    sp.dma_start(qs[rows, 0], heads.rearrange("(h d) s -> d h s", d=HD)).then_inc(s_in, 16)
                    for x in range(2):
                        sp.dma_start(vs[HD * x:HD * x + HD, 0, kv, :],
                                     dram["vT_b"][rows, SEQ:T]).then_inc(s_in, 16)
                sp.dma_start(ks[:, 0, 0, :], dram["kT_b"][:, SEQ:T]).then_inc(s_in, 16)
                sp.dma_start(sink[:, :], dram["sink_rows"]).then_inc(s_in, 16)
            for dst, name in ((ident[:, :], "ident"), (diag[:, :], f"diag{layer}"), (sel_b[:, :], "sel_b"),
                              (sel_h[:, :], "sel_h"), (own[:, :, :], "own"), (own_x[:, :, :, :], "own_x")):
                sp.dma_start(dst, dram[name]).then_inc(s_in, 16)
            for i, (g, b) in enumerate(units):
                need(sp, s_sc, i - RING + 1)
                sp.dma_start(kb[:, i % RING, :, 0:KEYS], dram[f"k_dec{layer}"][g * NS + b]).then_inc(k_in[i % RING], 16)
            for i, (g, b) in enumerate(vunits):
                need(sp, s_pv, i - RING + 1)
                if layer == 0:
                    src = dram[f"cache{g}"][b, 1].rearrange("(k s) f -> k s f", s=DIL[g])[:, 0, :]
                else:
                    src = dram["cache_b"][b, 1]
                sp.dma_start(vb[:, i % RING, :], src).then_inc(v_in[i % RING], 16)
            sp.wait_ge(s_ot, 1)
            sp.dma_start(dram["o_scr"].rearrange("(m p) s -> p m s", p=P)[:, :, SEQ:T], ot[:, :, :]).then_inc(s_out, 16)
            sp.wait_ge(s_out, 16)

        @block.gpsimd
        def _(pool):
            pool.memset(qbd[:, :, :, :, :], 0.0).then_inc(s_z, 1)
            pool.memset(probs[:, :, :], 0.0).then_inc(s_z, 1)
            pool.wait_ge(s_in, 16 * n_in)
            for i, (g, b) in enumerate(units):
                need(pool, s_sc, i - RING + 1)
                pool.tensor_copy(kb[:, i % RING, :, KEYS], ks[:, g, :, b]).then_inc(s_kn, 1)

        @block.scalar
        def _(act):
            for half in range(2):
                act.wait_ge(s_min, half + 1)
                lo = 1 if layer else 0
                act.activation(probs[:, half, lo:], banks[half][:, lo:ng * kc], ACT.Exp, scale=-1.0,
                               bias=nmx[:, half:half + 1], accum_out=den[:, half:half + 1]).then_inc(s_exp, 1)
                if layer:
                    act.activation(es[:, half:half + 1], ts[:, half:half + 1], ACT.Exp).then_inc(s_es, 1)
            for half in range(2):
                for g in range(ng):
                    act.wait_ge(s_tr, half * ng + g + 1)
                    act.copy(pts[:, half, g, :], banks[2 + (half * ng + g) % 2][:, 0:P]).then_inc(s_pts, 1)

        @block.vector
        def _(dve):
            dve.wait_ge(s_in, 16 * n_in)
            dve.wait_ge(s_z, 2)
            for g in range(ng):
                for h in range(2):
                    rows = slice(HD * h, HD * h + HD)
                    if layer == 0:
                        dst = qbd[rows, g].rearrange("r b p c -> r b (p c)")[:, :, h:h + 34 * (PAIRS - 1) + 1:34]
                    else:
                        dst = qbd[rows, 0, :, 0, GQA_B * h:GQA_B * h + GQA_B]
                    last = dve.tensor_copy(dst, qs[rows, g].rearrange("r m s -> r s m"))
            last.then_inc(s_qbd, 1)
            nd = [0]

            def step(ins):
                nd[0] += 1
                ins.then_inc(s_dn, 1)
                dve.wait_ge(s_dn, nd[0])

            lo = 1 if layer else 0
            for half in range(2):
                dve.wait_ge(s_sc, len(units) if half else len(units) - 4)
                col = slice(half, half + 1)
                last = dve.tensor_reduce(nmx[:, col], banks[half][:, lo:ng * kc], op=ALU.min, axis=AX_X)
                if layer:
                    step(last)
                    step(dve.tensor_scalar(ts[:, col], sink[:, :], -1.0, None, ALU.mult))
                    step(dve.tensor_tensor(nmx[:, col], nmx[:, col], ts[:, col], ALU.min))
                    last = dve.tensor_tensor(ts[:, col], nmx[:, col], sink[:, :], ALU.add)
                last.then_inc(s_min, 1)
            for half in range(2):
                col = slice(half, half + 1)
                dve.wait_ge(s_exp, half + 1)
                if layer:
                    dve.wait_ge(s_es, half + 1)
                    step(dve.tensor_tensor(den[:, col], den[:, col], es[:, col], ALU.add))
                step(dve.reciprocal(den[:, col], den[:, col]))
                dve.tensor_scalar(probs[:, half, :], probs[:, half, :], den[:, col], None, ALU.mult).then_inc(s_norm, 1)
            dve.wait_ge(s_norm, 2)
            for half in range(2):
                for g in range(ng):
                    last = dve.tensor_scalar(dn[:, half, g], own[:, :, :],
                                             probs[:, half, g * kc + KEYS:g * kc + KEYS + 1], None, ALU.mult)
            last.then_inc(s_new, 1)
            for half in range(2):
                dve.wait_ge(s_pv, len(vunits) // 2 * (half + 1))
                for i in range(vw // 512 or 1):
                    w = min(512, vw)
                    cols = slice(512 * i, 512 * i + w)
                    src = banks[4 + 2 * half + i][:, 0:w]
                    if layer == 0:
                        last = dve.tensor_tensor(om[:, half, cols], src, diag[:, cols], ALU.mult)
                    else:
                        step(dve.tensor_tensor(om[:, half, cols], src, diag[:, cols], ALU.mult))
                        last = dve.tensor_reduce(om2[:, half, :],
                                                 om[:, half, :].rearrange("p (k d) -> p d k", k=NKV_B),
                                                 op=ALU.add, axis=AX_X)
                last.then_inc(s_om, 1)
            dve.wait_ge(s_fin, 2)
            n_g = ng * PAIRS * NS
            step(dve.tensor_copy(pn[:, :, :, :].rearrange("p g m s -> p (g m s)"), banks[3][:, 0:n_g]))
            step(dve.tensor_copy(ot[:, :, :].rearrange("p m s -> p (m s)"), banks[2][:, 0:PAIRS * NS]))
            for g in range(ng):
                if layer == 0:
                    v_new = vs[:, g]
                    step(dve.tensor_tensor(ot2[:, :, :], pn[:, g], v_new, ALU.mult))
                else:
                    half_p = PAIRS // NKV_B
                    for kv in range(NKV_B):
                        sl = slice(kv * half_p, (kv + 1) * half_p)
                        ins = dve.tensor_tensor(ot2[:, sl, :], pn[:, 0, sl, :],
                                                vs[:, 0, kv, :].unsqueeze(1).broadcast_to((P, half_p, NS)), ALU.mult)
                    step(ins)
                ins = dve.tensor_tensor(ot[:, :, :], ot[:, :, :], ot2[:, :, :], ALU.add)
                if g < ng - 1:
                    step(ins)
            ins.then_inc(s_ot, 1)

        @block.tensor
        def _(pe):
            pe.wait_ge(s_qbd, 1)
            for i, (g, b) in enumerate(units):
                pe.wait_ge(k_in[i % RING], 16 * (i // RING + 1))
                pe.wait_ge(s_kn, i + 1)
                rows = slice(32 * (b % 4), 32 * (b % 4) + 32)
                for m in range(kp):
                    last = pe.matmul(banks[b // 4][rows, g * kc:(g + 1) * kc], qbd[:, g, b, m, :],
                                     kb[:, i % RING, m, :], start=(m == 0), stop=(m == kp - 1))
                last.then_inc(s_sc, 1)
            for half in range(2):
                for g in range(ng):
                    k = half * ng + g
                    pe.wait_ge(s_norm, half + 1)
                    need(pe, s_pts, k - 1)
                    pe.transpose(banks[2 + k % 2][:, 0:P], probs[:, half, g * kc:g * kc + KEYS], ident[:, :]
                                 ).then_inc(s_tr, 1)
            pe.wait_ge(s_pts, 2 * ng)
            for i, (g, b) in enumerate(vunits):
                pe.wait_ge(v_in[i % RING], 16 * (i // RING + 1))
                rows = slice(32 * (b % 4), 32 * (b % 4) + 32)
                for j in range(vw // 512 or 1):
                    w = min(512, vw)
                    last = pe.matmul(banks[4 + 2 * (b // 4) + j][rows, 0:w], pts[:, b // 4, g, rows],
                                     vb[:, i % RING, 512 * j:512 * j + w], start=(g == 0), stop=(g == ng - 1))
                last.then_inc(s_pv, 1)
            pe.wait_ge(s_new, 1)
            for half in range(2):
                for g in range(ng):
                    dst = banks[3][:, g * PAIRS * NS:(g + 1) * PAIRS * NS].rearrange("p (m s) -> p m s", s=NS)
                    last = pe.matmul(dst[:, :, 4 * half:4 * half + 4], sel_h[:, :], dn[:, half, g], start=True, stop=True)
            last.then_inc(s_fin, 1)
            for half in range(2):
                pe.wait_ge(s_om, half + 1)
                dst = banks[2][:, 0:PAIRS * NS].rearrange("p (m s) -> p m s", s=NS)
                if layer == 0:
                    for m in range(PAIRS):
                        last = pe.matmul(dst[:, m, 4 * half:4 * half + 4], om[:, half, m * P:(m + 1) * P], sel_b[:, :],
                                         start=True, stop=True)
                else:
                    for x in range(2):
                        rows = slice(HD * x, HD * x + HD)
                        last = pe.matmul(dst[rows, :, 4 * half:4 * half + 4], om2[:, half, :], own_x[:, x],
                                         start=True, stop=True)
            last.then_inc(s_fin, 1)


def roll_views(dram):
    views = []
    for g in range(NG):
        src, dst = dram[f"cache{g}"], dram[f"roll{g}"]
        for b in range(NS):
            for kv in range(2):
                views.append((dst[b, kv], src[b, kv, 1:, :]))
    for b in range(NS):
        for kv in range(2):
            views.append((dram["roll_b"][b, kv], dram["cache_b"][b, kv, 1:, :]))
    for layer in range(2):
        views.append((dram["roll_ffn"][layer], dram["ffn_rows"][layer, :, 1, :]))
    return [(cut(d), cut(s)) for d, s in views]


def cut(ap):
    return ap


def build(nc, dram):
    x_hi = nc.alloc_sbuf_tensor("x_hi", [P, KT, T], F32R)
    x_lo = nc.alloc_sbuf_tensor("x_lo", [P, KT, T], F32R)
    s_roll = nc.alloc_semaphore("rolled")

    views = roll_views(dram)
    with nc.Block() as block:
        @block.gpsimd
        def _(pool):
            for dst, src in views:
                pool.dma_start(dst, src).then_inc(s_roll, 16)

    mixer_a(nc, x_hi, x_lo, dram)
    for layer in range(2):
        if layer:
            mixer_b(nc, x_hi, x_lo, dram)
        decode(nc, dram, layer)
        names = {"w_o": f"w_o{layer}", "w_up": f"w_up{layer}", "w_down": f"w_down{layer}"}
        trunk(nc, x_hi, x_lo, {**dram, **{k: dram[v] for k, v in names.items()}}, layer)

    with nc.Block() as block:
        @block.sync
        def _(sp):
            sp.wait_ge(s_roll, 16 * len(views))


def shape_constants():
    f = np.float32
    pos = np.concatenate([np.arange(SEQ), np.full(NS, PAST)]).astype(f)
    inv = (f(THETA) ** (-np.arange(ROT // 2, dtype=f) * f(2.0) / f(ROT))).astype(f)
    ang = (pos[:, None] * inv[None, :]).astype(f)
    c, s = np.cos(ang).astype(f).T, np.sin(ang).astype(f).T
    cos, sin = np.ones((P, T), f), np.zeros((P, T), f)
    half = ROT // 2
    for h in (0, HD):
        cos[h:h + half], cos[h + half:h + ROT] = c, c
        sin[h:h + half], sin[h + half:h + ROT] = -s, s
    i, q = np.arange(P)[:, None], np.arange(P)[None, :]
    big = f(BIG)
    cur = np.where(q <= i, f(0), big)
    out = dict(
        cos=cos, sin=sin, ident=np.eye(P, dtype=f),
        mask_a=np.concatenate([np.where(q >= i, f(0), big), cur], 1).astype(f),
        mask_b=np.concatenate([np.where(q > i, f(0), big), cur], 1).astype(f),
        mask_c=np.where((q <= i) & (q // HD == i // HD), f(0), big).astype(f))
    sel = np.zeros((2 * QT, QT, P), f)
    for r in range(2 * QT):
        sel[r, r % QT, HD * (r // QT):HD * (r // QT) + HD] = 1
    out["sel"] = sel.reshape(2 * QT, QT * P)
    row = np.arange(P)
    h, b4, real = row % 32, row // 32, row % 32 < NH
    out["diag0"] = ((np.arange(D)[None] // HD == h[:, None]) & real[:, None]).astype(f)
    out["diag1"] = ((np.arange(P)[None] // HD == (h // GQA_B)[:, None]) & real[:, None]).astype(f)
    out["sel_b"] = ((b4[:, None] == np.arange(4)) & real[:, None]).astype(f)
    out["sel_h"] = ((h[:, None] % 2 == np.arange(P)[None] // HD) & real[:, None]).astype(f)
    pairs, seqs = np.arange(PAIRS)[None, :, None], np.arange(4)[None, None, :]
    own = lambda want: ((b4[:, None, None] == seqs) & want & real[:, None, None]).astype(f)
    out["own"] = own((h // 2)[:, None, None] == pairs)
    out["own_x"] = np.stack([own(h[:, None, None] == 2 * pairs + x) for x in range(2)], 1)
    return {k: np.ascontiguousarray(v) for k, v in out.items()}


def weight_blocks(w):
    k, n = w.shape
    return w.reshape(k // P, P, n // P, P).transpose(2, 1, 0, 3).reshape(n // P, P, k)


def feature_tiles(v):
    return np.moveaxis(v.reshape(v.shape[:-1] + (-1, P)), (-1, -2), (0, 1))


def lay_out(x_prompt, x_sample, cache_a1, cache_a2, cache_a3, cache_b, state_ffn, w_qkv_a, w_o_a, w_qkv_b,
            b_qkv_b, sinks_b, w_o_b, b_o_b, w_up, conv_w, conv_b, w_down, ln_g, ln_b):
    ins = shape_constants()
    ins["xT"] = np.concatenate([x_prompt[0], x_sample[:, 0]], 0).T
    w = w_qkv_a[0].reshape(KT, P, NG, 3, PAIRS, P)[:, :, :, [1, 0, 2]]
    ins["w_a"] = w.transpose(4, 2, 3, 1, 0, 5).reshape(PAIRS * NG * 3, P, D)
    for g, cache in enumerate((cache_a1, cache_a2, cache_a3)):
        ins[f"cache{g}"] = cache[0].reshape(NS, 2, cache.shape[3], D)
    ins["cache_b"] = cache_b[0].reshape(NS, 2, KEYS, NKV_B * HD)
    ins["k_dec0"] = np.concatenate([
        ins[f"cache{g}"][:, 0, ::DIL[g]].reshape(NS, KEYS, KT, P).transpose(0, 3, 2, 1) for g in range(NG)])
    ins["k_dec1"] = ins["cache_b"][:, 0].transpose(0, 2, 1)[:, :, None, :]
    wq, wk, wv = np.split(w_qkv_b[0], (NH * HD, NH * HD + P), axis=1)
    bq, bk, bv = np.split(b_qkv_b[0], (NH * HD, NH * HD + P))
    twice = lambda a, kv: np.concatenate([a[..., HD * kv:HD * kv + HD]] * 2, -1)
    ins["w_b"] = weight_blocks(np.concatenate([twice(wk, 0), twice(wk, 1), wv, wq], 1))
    ins["bias_b"] = feature_tiles(np.concatenate([twice(bk, 0), twice(bk, 1), bv, bq]))
    ins["sinks"] = sinks_b[0]
    ins["sink_rows"] = np.tile(np.pad(sinks_b[0], (0, 32 - NH)), 4)[:, None]
    ins["bias_o"] = np.stack([np.zeros((P, KT), np.float32), feature_tiles(b_o_b[0])])
    for layer, w_o in enumerate((w_o_a[0], w_o_b[0])):
        ins[f"w_o{layer}"] = weight_blocks(w_o)
        up = weight_blocks(w_up[layer]).reshape(2, FT, P, D).transpose(1, 0, 2, 3)
        ins[f"w_up{layer}"] = up.reshape(2 * FT, P, D)
        down = np.zeros((KT, P, 3 * D), np.float32)
        down[:, :, :DFF] = weight_blocks(w_down[layer])
        ins[f"w_down{layer}"] = down.reshape(KT, P, 3, D).transpose(0, 2, 1, 3).reshape(3 * KT, P, D)
    ins["taps"] = np.stack([feature_tiles(np.concatenate([conv_w[i], conv_b[i][None]])) for i in range(2)])
    ins["state"] = np.stack([feature_tiles(state_ffn[i].transpose(1, 0, 2)) for i in range(2)])
    ins["ffn_rows"] = state_ffn
    ins["ln"] = np.stack([feature_tiles(np.stack([ln_g[i], ln_b[i]], 1)).transpose(0, 2, 3, 1) for i in range(2)])
    return {k: np.ascontiguousarray(v) for k, v in ins.items()}


OUTPUTS = {
    "yT": (D, T), "kT": (NG, D, T), "vT": (NG, D, T), "kT_b": (P, T), "vT_b": (P, T), "gT": (2, P, FT, 2 + NS),
    "roll0": (NS, 2, 127, D), "roll1": (NS, 2, 511, D), "roll2": (NS, 2, 2047, D), "roll_b": (NS, 2, KEYS - 1, P),
    "roll_ffn": (2, NS, DFF)}
SCRATCH = {"st_scr": (96, P), "q_s": (NG, D, NS), "q_sb": (D, NS), "o_scr": (D, T)}


def kernel(**inputs):
    import concourse.bacc as bacc
    from concourse.bass_utils import run_bass_kernel_spmd

    ins = lay_out(**{k: np.asarray(v) for k, v in inputs.items()})
    nc = bacc.Bacc("TRN2", target_bir_lowering=False, num_devices=1)
    dram = {k: nc.dram_tensor(k, v.shape, F32, kind="ExternalInput").ap() for k, v in ins.items()}
    dram.update({k: nc.dram_tensor(k, s, F32, kind="ExternalOutput").ap() for k, s in OUTPUTS.items()})
    dram.update({k: nc.dram_tensor(k, s, F32, kind="Internal").ap() for k, s in SCRATCH.items()})
    build(nc, dram)
    r = run_bass_kernel_spmd(nc, [ins], core_ids=[0]).results[0]

    outs = [r["yT"][:, :SEQ].T[None], r["yT"][:, SEQ:].T[:, None]]
    for g, (win, dil) in enumerate(GROUPS):
        v_tok = r["vT"][g][:, :SEQ].reshape(D, dil, SEQ // dil).transpose(0, 2, 1).reshape(D, SEQ)
        keep = min(win, SEQ)
        prompt = np.stack([r["kT"][g][:, SEQ - keep:SEQ].T, v_tok[:, SEQ - keep:].T])
        outs.append(prompt.reshape(1, 1, 2, keep, NH, HD))
        new = np.stack([r["kT"][g][:, SEQ:].T, r["vT"][g][:, SEQ:].T], 1)[:, :, None]
        outs.append(np.concatenate([r[f"roll{g}"], new], 2).reshape(1, NS, 2, -1, NH, HD))
    prompt = np.stack([r["kT_b"][:, SEQ - KEYS:SEQ].T, r["vT_b"][:, SEQ - KEYS:SEQ].T])
    outs.append(prompt.reshape(1, 1, 2, KEYS, NKV_B, HD))
    new = np.stack([r["kT_b"][:, SEQ:].T, r["vT_b"][:, SEQ:].T], 1)[:, :, None]
    outs.append(np.concatenate([r["roll_b"], new], 2).reshape(1, NS, 2, KEYS, NKV_B, HD))
    g_rows = r["gT"].transpose(0, 3, 2, 1).reshape(2, 2 + NS, DFF)
    outs.append(g_rows[:, None, :2])
    outs.append(np.stack([r["roll_ffn"], g_rows[:, 2:]], 2))
    return tuple(np.ascontiguousarray(x) for x in outs)
```
